# Optimizing a Trainium2 kernel written in Bass

```python
import math
import jax, jax.numpy as jnp
from jax import lax
import numpy as np

D_MODEL = 1024
BATCH = 1
SEQ = 256
DEPTH = 1

GRID_W = 64
CTX_LEN = 256

N_MOD = 6
NORM_EPS = 1e-6

MIX_WIDTH = D_MODEL
RET_HEADS = 4
RET_WIDTH = MIX_WIDTH // 2
RET_DV = RET_WIDTH // RET_HEADS
RET_DK = RET_DV // 2
RET_CHUNK = 128
DIFF_HEADS = 4
DIFF_WIDTH = MIX_WIDTH - RET_WIDTH
DIFF_DV = DIFF_WIDTH // DIFF_HEADS
DIFF_D = DIFF_DV // 2
Q_BLOCK = 128
ROPE_DIM = RET_DK
ROPE_BASE = 10000.0

RET_QK_COLS = RET_HEADS * RET_DK
IN_SPLITS = (RET_QK_COLS, 2 * RET_QK_COLS, 2 * RET_QK_COLS + RET_WIDTH, 2 * RET_QK_COLS + 2 * RET_WIDTH, 2 * RET_QK_COLS + 2 * RET_WIDTH + DIFF_WIDTH, 2 * RET_QK_COLS + 2 * RET_WIDTH + 2 * DIFF_WIDTH)
IN_COLS = 2 * RET_QK_COLS + 2 * RET_WIDTH + 3 * DIFF_WIDTH

PEER_HEADS = 8
PEER_NKEYS = 128
PEER_N_EXPERTS = PEER_NKEYS * PEER_NKEYS
PEER_QDIM = 256
PEER_HALF = PEER_QDIM // 2
PEER_TOPK = 16
PEER_BLOCK = 128


def rms_norm(x, g, eps=NORM_EPS):
    xf = x.astype(jnp.float32)
    y = xf * lax.rsqrt(jnp.mean(xf * xf, axis=-1, keepdims=True) + eps)
    return (y * g.astype(jnp.float32)).astype(x.dtype)

def modulate(x, g, shift, scale):
    return rms_norm(x, g) * (1.0 + scale) + shift

def adaln_params(cond, w_mod, b_mod):
    mod = jax.nn.silu(cond) @ w_mod + b_mod
    return mod.reshape(cond.shape[0], N_MOD, 1, cond.shape[-1])

def heads(t, n_heads):
    b, l, _ = t.shape
    return t.reshape(b, l, n_heads, -1).transpose(0, 2, 1, 3)

def merge_heads(t):
    b, h, l, e = t.shape
    return t.transpose(0, 2, 1, 3).reshape(b, l, h * e)

def axial_rope_tables(rows, head_dim, dtype):
    quarter = head_dim // 4
    freqs = ROPE_BASE ** (-jnp.arange(quarter, dtype=jnp.float32) / quarter)
    row = jnp.repeat(jnp.arange(rows, dtype=jnp.float32), GRID_W)
    col = jnp.tile(jnp.arange(GRID_W, dtype=jnp.float32), rows)
    ar = row[:, None] * freqs
    ac = col[:, None] * freqs
    ang = jnp.concatenate([ar, ar, ac, ac], axis=-1)
    return jnp.cos(ang).astype(dtype), jnp.sin(ang).astype(dtype)

def apply_rope(x, cos, sin):
    quarter = x.shape[-1] // 4
    xr = x.reshape(x.shape[:-1] + (2, 2, quarter))
    rot = jnp.concatenate([-xr[..., 1:, :], xr[..., :1, :]], axis=-2).reshape(x.shape)
    return x * cos + rot * sin

def decayed_state(k, v, log_gamma):
    l = k.shape[2]
    dist = (l - 1 - jnp.arange(l)).astype(jnp.float32)
    w = jnp.exp(dist[None, :] * log_gamma[:, None]).astype(k.dtype)
    return jnp.einsum('bhjd,hj,bhje->bhde', k, w, v)

def retention_chunkwise(q, k, v, log_gamma, init_state, strict):
    b, h, l, dk = q.shape
    dv = v.shape[-1]
    n = l // RET_CHUNK
    C = RET_CHUNK
    qc = q.reshape(b, h, n, C, dk)
    kc = k.reshape(b, h, n, C, dk)
    vc = v.reshape(b, h, n, C, dv)
    idx = jnp.arange(C, dtype=jnp.float32)
    diff = idx[:, None] - idx[None, :]
    mask = (diff > 0) if strict else (diff >= 0)
    lg = log_gamma[:, None, None]
    intra_decay = jnp.where(mask, jnp.exp(jnp.where(mask, diff, 0.0) * lg), 0.0).astype(q.dtype)
    scores = jnp.einsum('bhnid,bhnjd->bhnij', qc, kc) * intra_decay[None, :, None]
    out = jnp.einsum('bhnij,bhnje->bhnie', scores, vc)
    k_w = jnp.exp((C - 1 - idx)[None, :] * log_gamma[:, None]).astype(q.dtype)
    local = jnp.einsum('bhnjd,hj,bhnje->bhnde', kc, k_w, vc)
    chunk_decay = jnp.exp(C * log_gamma).astype(q.dtype)[None, :, None, None]

    def step(r, s):
        return chunk_decay * r + s, r

    _, r_prev = lax.scan(step, init_state.astype(local.dtype), jnp.moveaxis(local, 2, 0))
    r_prev = jnp.moveaxis(r_prev, 0, 2)
    q_w = jnp.exp((idx + 1.0)[None, :] * log_gamma[:, None]).astype(q.dtype)
    out = out + jnp.einsum('bhnid,hi,bhnde->bhnie', qc, q_w, r_prev)
    return out.reshape(b, h, l, dv)

def bidirectional_retention(q, k, v, lg_f, lg_b, state_f, state_b):
    flip = lambda t: jnp.flip(t, axis=2)
    y_f = retention_chunkwise(q, k, v, lg_f, state_f, strict=False)
    y_b = flip(retention_chunkwise(flip(q), flip(k), flip(v), lg_b, state_b, strict=True))
    return y_f + y_b

def retention_group(rq, rk, rv, rg, crq, crk, crv, crg, decay_logit, norm_g, cos, sin, with_ctx_out):
    scale = RET_DK ** -0.5
    log_gamma = jax.nn.log_sigmoid(decay_logit.astype(jnp.float32))
    lg_f, lg_b = log_gamma[0], log_gamma[1]
    q = apply_rope(heads(rq, RET_HEADS), cos, sin)
    k = apply_rope(heads(rk, RET_HEADS), cos, sin) * scale
    v = heads(rv, RET_HEADS)
    kc = heads(crk, RET_HEADS) * scale
    vc = heads(crv, RET_HEADS)
    state_f = decayed_state(kc, vc, lg_f)
    state_b = decayed_state(jnp.flip(kc, axis=2), jnp.flip(vc, axis=2), lg_b)
    y = bidirectional_retention(q, k, v, lg_f, lg_b, state_f, state_b)
    g_norm = norm_g[:, None, :]
    out = merge_heads(rms_norm(y, g_norm)) * jax.nn.silu(rg)
    ctx_out = None
    if with_ctx_out:
        qc = heads(crq, RET_HEADS)
        zero = jnp.zeros(state_f.shape, state_f.dtype)
        yc = bidirectional_retention(qc, kc, vc, lg_f, lg_b, zero, zero)
        ctx_out = merge_heads(rms_norm(yc, g_norm)) * jax.nn.silu(crg)
    return out, ctx_out

def diff_softmax_attend(q, k, v, lam):
    s = jnp.einsum('bhpqd,bhpkd->bhpqk', q, k).astype(jnp.float32) * (DIFF_D ** -0.5)
    p = jax.nn.softmax(s, axis=-1)
    a = (p[:, :, 0] - lam * p[:, :, 1]).astype(v.dtype)
    return jnp.einsum('bhqk,bhke->bhqe', a, v)

def diff_attention_group(dq, dk, dv, cdq, cdk, cdv, qk_norm_g, lam_params, norm_g, lam_init, cos, sin, with_ctx_out):
    def qk_heads(t, g):
        b_, l_, _ = t.shape
        t = t.reshape(b_, l_, DIFF_HEADS, 2, DIFF_D).transpose(0, 2, 3, 1, 4)
        return rms_norm(t, g)

    q = apply_rope(qk_heads(dq, qk_norm_g[0]), cos, sin)
    k = apply_rope(qk_heads(dk, qk_norm_g[1]), cos, sin)
    v = heads(dv, DIFF_HEADS)
    kc = qk_heads(cdk, qk_norm_g[1])
    vc = heads(cdv, DIFF_HEADS)
    lp = lam_params.astype(jnp.float32)
    lam = jnp.exp(jnp.sum(lp[0] * lp[1])) - jnp.exp(jnp.sum(lp[2] * lp[3])) + lam_init
    keys = jnp.concatenate([kc, k], axis=3)
    vals = jnp.concatenate([vc, v], axis=2)
    b, h, _, l, d = q.shape
    nb = l // Q_BLOCK
    q_blocks = jnp.moveaxis(q.reshape(b, h, 2, nb, Q_BLOCK, d), 3, 0)
    y = lax.map(lambda qb: diff_softmax_attend(qb, keys, vals, lam), q_blocks)
    y = jnp.moveaxis(y, 0, 2).reshape(b, h, l, DIFF_DV)
    g_norm = norm_g[:, None, :]
    out = merge_heads(rms_norm(y, g_norm) * (1.0 - lam_init))
    ctx_out = None
    if with_ctx_out:
        qc = qk_heads(cdq, qk_norm_g[0])
        yc = diff_softmax_attend(qc, kc, vc, lam)
        ctx_out = merge_heads(rms_norm(yc, g_norm) * (1.0 - lam_init))
    return out, ctx_out

def peer_ffn(h, w_query, sub_keys, expert_u, expert_v):
    b, l, d = h.shape
    tokens = h.reshape(-1, PEER_BLOCK, d)

    def block_fn(hb):
        t = hb.shape[0]
        q = (hb @ w_query).reshape(t, PEER_HEADS, 2, PEER_HALF)
        s = jnp.einsum('thpc,hpnc->thpn', q, sub_keys).astype(jnp.float32)
        v1, i1 = lax.top_k(s[:, :, 0], PEER_TOPK)
        v2, i2 = lax.top_k(s[:, :, 1], PEER_TOPK)
        cand = (v1[..., :, None] + v2[..., None, :]).reshape(t, PEER_HEADS, PEER_TOPK * PEER_TOPK)
        cand_idx = (i1[..., :, None] * PEER_NKEYS + i2[..., None, :]).reshape(t, PEER_HEADS, PEER_TOPK * PEER_TOPK)
        best, pos = lax.top_k(cand, PEER_TOPK)
        experts = jnp.take_along_axis(cand_idx, pos, axis=-1)
        gate = jax.nn.softmax(best, axis=-1).astype(hb.dtype)
        u = expert_u[experts]
        vsel = expert_v[experts]
        act = jax.nn.gelu(jnp.einsum('thkd,td->thk', u, hb), approximate=False)
        return jnp.einsum('thk,thkd->td', gate * act, vsel)

    return lax.map(block_fn, tokens).reshape(b, l, d)

def first_inputs(seed: int = 0) -> dict:
    key = jax.random.key(seed)
    ks = jax.random.split(key, 20)
    nrm = lambda k, shape, s: jax.random.normal(k, shape, jnp.float32) * s
    L = DEPTH
    D = D_MODEL
    decay_init = jnp.asarray(np.log(2.0 ** (5 + np.arange(RET_HEADS)) - 1.0).astype(np.float32))
    return {
        "x": nrm(ks[0], (BATCH, SEQ, D), 1.0),
        "c": nrm(ks[1], (BATCH, D), 1.0),
        "ctx": nrm(ks[2], (BATCH, CTX_LEN, D), 1.0),
        "c_ctx": nrm(ks[3], (D,), 1.0),
        "w_mod": nrm(ks[4], (L, D, N_MOD * D), 0.5 * D ** -0.5),
        "b_mod": nrm(ks[5], (L, N_MOD * D), 0.02),
        "norm1_g": 1.0 + nrm(ks[6], (L, D), 0.02),
        "norm2_g": 1.0 + nrm(ks[7], (L, D), 0.02),
        "w_in": nrm(ks[8], (L, D, IN_COLS), D ** -0.5),
        "ret_decay_logit": decay_init[None, None, :] + nrm(ks[9], (L, 2, RET_HEADS), 0.1),
        "ret_norm_g": 1.0 + nrm(ks[10], (L, RET_HEADS, RET_DV), 0.02),
        "diff_qk_norm_g": 1.0 + nrm(ks[11], (L, 2, DIFF_D), 0.02),
        "diff_lambda": nrm(ks[12], (L, 4, DIFF_D), 0.1),
        "diff_norm_g": 1.0 + nrm(ks[13], (L, DIFF_HEADS, DIFF_DV), 0.02),
        "w_out": nrm(ks[14], (L, MIX_WIDTH, D), MIX_WIDTH ** -0.5),
        "peer_w_query": nrm(ks[15], (L, D, PEER_HEADS * PEER_QDIM), D ** -0.5),
        "peer_sub_keys": nrm(ks[16], (L, PEER_HEADS, 2, PEER_NKEYS, PEER_HALF), PEER_HALF ** -0.5),
        "peer_u": nrm(ks[17], (L, PEER_N_EXPERTS, D), D ** -0.5),
        "peer_v": nrm(ks[18], (L, PEER_N_EXPERTS, D), (PEER_HEADS * PEER_TOPK) ** -0.5),
    }

def first_block(x, c, ctx, c_ctx, w_mod, b_mod, norm1_g, norm2_g, w_in, ret_decay_logit, ret_norm_g, diff_qk_norm_g, diff_lambda, diff_norm_g, w_out, peer_w_query, peer_sub_keys, peer_u, peer_v):
    rows = x.shape[1] // GRID_W
    cos, sin = axial_rope_tables(rows, ROPE_DIM, x.dtype)
    for layer in range(DEPTH):
        last = layer == DEPTH - 1
        lam_init = 0.8 - 0.6 * math.exp(-0.3 * layer)
        mod = adaln_params(c, w_mod[layer], b_mod[layer])
        mod_c = adaln_params(c_ctx[None, :], w_mod[layer], b_mod[layer])
        h = modulate(x, norm1_g[layer], mod[:, 0], mod[:, 1])
        hc = modulate(ctx, norm1_g[layer], mod_c[:, 0], mod_c[:, 1])
        rq, rk, rv, rg, dq, dk, dv = jnp.split(h @ w_in[layer], IN_SPLITS, axis=-1)
        crq, crk, crv, crg, cdq, cdk, cdv = jnp.split(hc @ w_in[layer], IN_SPLITS, axis=-1)
        ret_lat, ret_ctx = retention_group(rq, rk, rv, rg, crq, crk, crv, crg, ret_decay_logit[layer], ret_norm_g[layer], cos, sin, not last)
        diff_lat, diff_ctx = diff_attention_group(dq, dk, dv, cdq, cdk, cdv, diff_qk_norm_g[layer], diff_lambda[layer], diff_norm_g[layer], lam_init, cos, sin, not last)
        x = x + mod[:, 2] * (jnp.concatenate([ret_lat, diff_lat], axis=-1) @ w_out[layer])
        h2 = modulate(x, norm2_g[layer], mod[:, 3], mod[:, 4])
        x = x + mod[:, 5] * peer_ffn(h2, peer_w_query[layer], peer_sub_keys[layer], peer_u[layer], peer_v[layer])
        if not last:
            ctx = ctx + mod_c[:, 2] * (jnp.concatenate([ret_ctx, diff_ctx], axis=-1) @ w_out[layer])
            hc2 = modulate(ctx, norm2_g[layer], mod_c[:, 3], mod_c[:, 4])
            ctx = ctx + mod_c[:, 5] * peer_ffn(hc2, peer_w_query[layer], peer_sub_keys[layer], peer_u[layer], peer_v[layer])
    return x


DEPTH_2 = 2

N_A = DEPTH_2 // 2
N_B = DEPTH_2 - N_A
CONV_W = 3
N_HEADS = 8
HEAD_DIM = D_MODEL // N_HEADS
BLOCK = 256
TOPK = 3
Q_CHUNK = 32
ROT_DIM = HEAD_DIM // 4
ROPE_THETA = 500000.0
MEM_LEN = 256
MEM_HEADS = 4
MEM_HEAD_DIM = D_MODEL // MEM_HEADS
D_FF = ((8 * D_MODEL + 3 * 256 - 1) // (3 * 256)) * 256
EPS = 1e-6


def rms_norm_2(x, g):
    x32 = x.astype(jnp.float32)
    y = x32 * lax.rsqrt(jnp.mean(x32 * x32, axis=-1, keepdims=True) + EPS)
    return (y * g.astype(jnp.float32)).astype(x.dtype)

def rope_cos_sin(positions):
    inv_freq = ROPE_THETA ** (-jnp.arange(0, ROT_DIM, 2, dtype=jnp.float32) / ROT_DIM)
    ang = positions.astype(jnp.float32)[..., None] * inv_freq
    return jnp.cos(ang)[:, :, None, :], jnp.sin(ang)[:, :, None, :]

def apply_partial_rope(x, cos, sin):
    xr = x[..., :ROT_DIM].astype(jnp.float32)
    x1, x2 = xr[..., : ROT_DIM // 2], xr[..., ROT_DIM // 2:]
    rot = jnp.concatenate([x1 * cos - x2 * sin, x2 * cos + x1 * sin], axis=-1)
    return jnp.concatenate([rot.astype(x.dtype), x[..., ROT_DIM:]], axis=-1)

def short_conv_mixer(h, w_in, w_conv, w_out):
    b_gate, c_gate, u = jnp.split(h @ w_in, 3, axis=-1)
    z = c_gate * u
    conv = lax.conv_general_dilated(
        z, w_conv[:, None, :].astype(z.dtype), window_strides=(1,),
        padding=[(CONV_W - 1, 0)], dimension_numbers=("NWC", "WIO", "NWC"),
        feature_group_count=D_MODEL)
    return (b_gate * conv) @ w_out

def mem_cross_attention(h, mem_n, w_q, w_kv, w_o):
    bsz, seq, _ = h.shape
    q = (h @ w_q).reshape(bsz, seq, MEM_HEADS, MEM_HEAD_DIM)
    k, v = jnp.split(mem_n @ w_kv, 2, axis=-1)
    k = k.reshape(bsz, -1, MEM_HEADS, MEM_HEAD_DIM)
    v = v.reshape(bsz, -1, MEM_HEADS, MEM_HEAD_DIM)
    s = jnp.einsum("bshd,bmhd->bhsm", q, k).astype(jnp.float32) * (MEM_HEAD_DIM ** -0.5)
    p = jax.nn.softmax(s, axis=-1).astype(v.dtype)
    o = jnp.einsum("bhsm,bmhd->bshd", p, v).reshape(bsz, seq, D_MODEL)
    return o @ w_o

def swiglu(h, w_gu, w_down):
    g, u = jnp.split(h @ w_gu, 2, axis=-1)
    return (jax.nn.silu(g) * u) @ w_down

def shared_kv(x, kv_norm, w_kv, cos, sin):
    bsz, seq, _ = x.shape
    n_blocks = -(-seq // BLOCK)
    pad = n_blocks * BLOCK - seq
    k, v = jnp.split(rms_norm_2(x, kv_norm) @ w_kv, 2, axis=-1)
    k = apply_partial_rope(k.reshape(bsz, seq, N_HEADS, HEAD_DIM), cos, sin)
    v = v.reshape(bsz, seq, N_HEADS, HEAD_DIM)
    k = jnp.pad(k, ((0, 0), (0, pad), (0, 0), (0, 0)))
    v = jnp.pad(v, ((0, 0), (0, pad), (0, 0), (0, 0)))
    k_blk = k.transpose(0, 2, 1, 3).reshape(bsz, N_HEADS, n_blocks, BLOCK, HEAD_DIM)
    v_blk = v.transpose(0, 2, 1, 3).reshape(bsz, N_HEADS, n_blocks, BLOCK, HEAD_DIM)
    k_mean = jnp.mean(k_blk.astype(jnp.float32), axis=3)
    return k_blk, v_blk, k_mean

def moba_attention(h, w_q, w_o, cos, sin, k_blk, v_blk, k_mean):
    bsz, seq, _ = h.shape
    n_blocks = k_blk.shape[2]
    k_sel = min(TOPK, n_blocks)
    n_chunks = seq // Q_CHUNK
    scale = HEAD_DIM ** -0.5
    q = apply_partial_rope((h @ w_q).reshape(bsz, seq, N_HEADS, HEAD_DIM), cos, sin)
    q_chunks = q.transpose(0, 2, 1, 3).reshape(bsz, N_HEADS, n_chunks, Q_CHUNK, HEAD_DIM)
    q_chunks = q_chunks.transpose(2, 0, 1, 3, 4)
    bi = jnp.arange(bsz)[:, None, None, None]
    hi = jnp.arange(N_HEADS)[None, :, None, None]

    def chunk_fn(args):
        c, q_c = args
        qpos = c * Q_CHUNK + jnp.arange(Q_CHUNK)
        qb = (c * Q_CHUNK) // BLOCK
        gate = jnp.einsum("bhqd,bhnd->bhqn", q_c.astype(jnp.float32), k_mean)
        past = jnp.arange(n_blocks) < qb
        gate = jnp.where(past[None, None, None, :], gate, -jnp.inf)
        _, idx = lax.top_k(gate, k_sel)
        valid = idx < qb
        kg = k_blk[bi, hi, idx]
        vg = v_blk[bi, hi, idx]
        s_sel = jnp.einsum("bhqd,bhqrkd->bhqrk", q_c, kg).astype(jnp.float32) * scale
        s_sel = jnp.where(valid[..., None], s_sel, -jnp.inf)
        s_sel = s_sel.reshape(bsz, N_HEADS, Q_CHUNK, k_sel * BLOCK)
        k_own = lax.dynamic_index_in_dim(k_blk, qb, axis=2, keepdims=False)
        v_own = lax.dynamic_index_in_dim(v_blk, qb, axis=2, keepdims=False)
        s_own = jnp.einsum("bhqd,bhkd->bhqk", q_c, k_own).astype(jnp.float32) * scale
        kpos = qb * BLOCK + jnp.arange(BLOCK)
        s_own = jnp.where((kpos[None, :] <= qpos[:, None])[None, None], s_own, -jnp.inf)
        p = jax.nn.softmax(jnp.concatenate([s_sel, s_own], axis=-1), axis=-1)
        p_sel = p[..., : k_sel * BLOCK].reshape(bsz, N_HEADS, Q_CHUNK, k_sel, BLOCK)
        p_own = p[..., k_sel * BLOCK:]
        o = jnp.einsum("bhqrk,bhqrkd->bhqd", p_sel.astype(vg.dtype), vg)
        o = o + jnp.einsum("bhqk,bhkd->bhqd", p_own.astype(v_own.dtype), v_own)
        return o

    out = lax.map(chunk_fn, (jnp.arange(n_chunks, dtype=jnp.int32), q_chunks))
    out = out.transpose(1, 0, 3, 2, 4).reshape(bsz, seq, D_MODEL)
    return out @ w_o

def second_inputs(seed: int = 0) -> dict:
    key = jax.random.key(seed)
    ks = jax.random.split(key, 24)
    f32 = jnp.float32

    def w(k, shape, fan_in):
        return jax.random.normal(k, shape, f32) * (fan_in ** -0.5)

    def gain(k, shape):
        return 1.0 + 0.02 * jax.random.normal(k, shape, f32)

    x = jax.random.normal(ks[0], (BATCH, SEQ, D_MODEL), f32)
    mem = jax.random.normal(ks[1], (BATCH, MEM_LEN, D_MODEL), f32)
    offset = jax.random.randint(ks[2], (BATCH, 1), 0, 8192, dtype=jnp.int32)
    positions = offset + jnp.arange(SEQ, dtype=jnp.int32)[None, :]
    return {
        "x": x,
        "mem": mem,
        "positions": positions,
        "norm_mix": gain(ks[3], (DEPTH_2, D_MODEL)),
        "norm_mem": gain(ks[4], (DEPTH_2, D_MODEL)),
        "norm_memkv": gain(ks[5], (DEPTH_2, D_MODEL)),
        "norm_ffn": gain(ks[6], (DEPTH_2, D_MODEL)),
        "norm_final": gain(ks[7], (D_MODEL,)),
        "conv_w_in": w(ks[8], (N_A, D_MODEL, 3 * D_MODEL), D_MODEL),
        "conv_w": w(ks[9], (N_A, CONV_W, D_MODEL), CONV_W),
        "conv_w_out": w(ks[10], (N_A, D_MODEL, D_MODEL), D_MODEL),
        "kv_norm": gain(ks[11], (D_MODEL,)),
        "w_kv": w(ks[12], (D_MODEL, 2 * D_MODEL), D_MODEL),
        "moba_w_q": w(ks[13], (N_B, D_MODEL, D_MODEL), D_MODEL),
        "moba_w_o": w(ks[14], (N_B, D_MODEL, D_MODEL), D_MODEL),
        "mem_w_q": w(ks[15], (DEPTH_2, D_MODEL, D_MODEL), D_MODEL),
        "mem_w_kv": w(ks[16], (DEPTH_2, D_MODEL, 2 * D_MODEL), D_MODEL),
        "mem_w_o": w(ks[17], (DEPTH_2, D_MODEL, D_MODEL), D_MODEL),
        "ffn_w_gu": w(ks[18], (DEPTH_2, D_MODEL, 2 * D_FF), D_MODEL),
        "ffn_w_down": w(ks[19], (DEPTH_2, D_FF, D_MODEL), D_FF),
    }

def second_block(x, mem, positions, norm_mix, norm_mem, norm_memkv, norm_ffn, norm_final,
              conv_w_in, conv_w, conv_w_out, kv_norm, w_kv, moba_w_q, moba_w_o,
              mem_w_q, mem_w_kv, mem_w_o, ffn_w_gu, ffn_w_down):
    cos, sin = rope_cos_sin(positions)
    k_blk = v_blk = k_mean = None
    for l in range(DEPTH_2):
        h = rms_norm_2(x, norm_mix[l])
        if l < N_A:
            x = x + short_conv_mixer(h, conv_w_in[l], conv_w[l], conv_w_out[l])
        else:
            j = l - N_A
            x = x + moba_attention(h, moba_w_q[j], moba_w_o[j], cos, sin, k_blk, v_blk, k_mean)
        x = x + mem_cross_attention(rms_norm_2(x, norm_mem[l]), rms_norm_2(mem, norm_memkv[l]),
                                    mem_w_q[l], mem_w_kv[l], mem_w_o[l])
        x = x + swiglu(rms_norm_2(x, norm_ffn[l]), ffn_w_gu[l], ffn_w_down[l])
        if l == N_A - 1:
            k_blk, v_blk, k_mean = shared_kv(x, kv_norm, w_kv, cos, sin)
    return rms_norm_2(x, norm_final)


def setup_inputs(seed=0):
    out = dict(first_inputs(seed))
    for name, value in second_inputs(seed + 1).items():
        if name != "x":
            out[name + "_2"] = value
    return out


def reference(
    x, c, ctx, c_ctx, w_mod, b_mod, norm1_g, norm2_g, w_in, ret_decay_logit, ret_norm_g,
    diff_qk_norm_g, diff_lambda, diff_norm_g, w_out, peer_w_query, peer_sub_keys, peer_u,
    peer_v, mem_2, positions_2, norm_mix_2, norm_mem_2, norm_memkv_2, norm_ffn_2, norm_final_2,
    conv_w_in_2, conv_w_2, conv_w_out_2, kv_norm_2, w_kv_2, moba_w_q_2, moba_w_o_2, mem_w_q_2,
    mem_w_kv_2, mem_w_o_2, ffn_w_gu_2, ffn_w_down_2,
):
    x = first_block(
        x, c, ctx, c_ctx, w_mod, b_mod, norm1_g, norm2_g, w_in, ret_decay_logit, ret_norm_g,
        diff_qk_norm_g, diff_lambda, diff_norm_g, w_out, peer_w_query, peer_sub_keys, peer_u,
        peer_v,
    )
    return second_block(
        x, mem_2, positions_2, norm_mix_2, norm_mem_2, norm_memkv_2, norm_ffn_2, norm_final_2,
        conv_w_in_2, conv_w_2, conv_w_out_2, kv_norm_2, w_kv_2, moba_w_q_2, moba_w_o_2,
        mem_w_q_2, mem_w_kv_2, mem_w_o_2, ffn_w_gu_2, ffn_w_down_2,
    )


_drawn_inputs = setup_inputs


def setup_inputs(seed=0):
    import zlib

    import numpy as np

    out = dict(_drawn_inputs(seed))
    spreads = {}
    factors = {'norm1_g': 5.726,
     'norm2_g': 8.0,
     'ret_norm_g': 8.0,
     'diff_qk_norm_g': 8.0,
     'diff_lambda': 4.098,
     'diff_norm_g': 8.0,
     'norm_mem_2': 8.0,
     'norm_memkv_2': 8.0,
     'norm_ffn_2': 3.593,
     'norm_final_2': 2.81,
     'kv_norm_2': 8.0}
    for name, (base, spread) in spreads.items():
        noise = np.random.default_rng([zlib.crc32(name.encode()), seed]).standard_normal(out[name].shape)
        drawn = base * np.exp(spread * noise) if base else spread * noise
        out[name] = __import__('jax').numpy.asarray(drawn.astype(out[name].dtype))
    for name, factor in factors.items():
        out[name] = (out[name] * factor).astype(out[name].dtype)
    return out
```

```python
import math
from contextlib import ExitStack

import concourse.bass as bass
import numpy as np
from concourse import mybir

ALU = mybir.AluOpType
ACT = mybir.ActivationFunctionType
F32 = mybir.dt.float32
I32 = mybir.dt.int32
U32 = mybir.dt.uint32
AX = mybir.AxisListType.X

P = 128
D = 1024
KC = D // P
NT = 2
TOK = NT * P
EPS = 1e-6
LAM_INIT = 0.8 - 0.6 * math.exp(-0.3 * 0)
RH, RDK, RDV = 4, 64, 128
DH, DD, DDV = 4, 64, 128
PH, PN, PK = 8, 128, 16
MH, BH = 4, 8
DFF = 2816
FC = DFF // P
ROT = 32
RING = 4
SLOTS = 8
NEG = -1e30
MINF = -3.0e38
TWO_PI = (6.28125, float(np.float32(np.floor((2 * math.pi - 6.28125) * 2.0 ** 20) / 2.0 ** 20)),
          2 * math.pi - 6.28125 - float(np.floor((2 * math.pi - 6.28125) * 2.0 ** 20) / 2.0 ** 20))
PI_F = 3.1415925

K_ID, K_COS, K_SIN, K_TRI, K_INV, K_IOTA, K_END = 0, 128, 256, 384, 512, 528, 544
C_C, C_CC, C_N1, C_N2, C_MIX, C_MEM, C_MKV, C_FFN, C_KV, C_CONV = 0, 8, 16, 24, 32, 48, 64, 80, 96, 104
C_BM, C_RN, C_DN = 128, 176, 180


def shape_constants():
    keep = np.zeros((P, K_END), np.float32)
    keep[:, K_ID:K_ID + P] = np.eye(P, dtype=np.float32)
    quarter = RDK // 4
    freqs = (np.float32(10000.0) ** (-np.arange(quarter, dtype=np.float32) / np.float32(quarter))).astype(np.float32)
    tok = np.arange(TOK)
    row, col = (tok // 64).astype(np.float32), (tok % 64).astype(np.float32)
    ar, ac = row[:, None] * freqs, col[:, None] * freqs
    ang = np.concatenate([ar, ar, ac, ac], -1)
    cos, sin = np.cos(ang).astype(np.float32), np.sin(ang).astype(np.float32)
    signed = sin.reshape(TOK, 2, 2, quarter) * np.array([-1.0, 1.0], np.float32)[None, None, :, None]
    keep[:, K_COS:K_COS + 128] = cos.reshape(NT, P, 64).transpose(1, 0, 2).reshape(P, 128)
    keep[:, K_SIN:K_SIN + 128] = signed.reshape(NT, P, 64).transpose(1, 0, 2).reshape(P, 128)
    q, k = np.arange(P)[:, None], np.arange(P)[None, :]
    keep[:, K_TRI:K_TRI + P] = np.where(k <= q, 0.0, NEG)
    keep[:, K_INV:K_INV + 16] = (np.float32(500000.0) ** (-np.arange(0, ROT, 2, dtype=np.float32) / np.float32(ROT)))
    keep[:, K_IOTA:K_IOTA + 16] = np.arange(16)
    j = np.arange(P)[:, None]
    i = np.arange(TOK)[None, :]
    dist = np.zeros((P, 4, 2, TOK), np.float32)
    for t in range(2):
        jj = t * P + j
        dist[:, 0, t] = i + TOK - jj
        dist[:, 1, t] = TOK - i + jj
        dist[:, 2, t] = np.maximum(i - jj, 0)
        dist[:, 3, t] = np.maximum(jj - i, 0)
    return keep, dist.reshape(P, 8 * TOK)


def weight_plan(a):
    plan = []

    def wide(name, w, n0=0, n1=None):
        n1 = w.shape[1] if n1 is None else n1
        for i, n in enumerate(range(n0, n1, 512)):
            plan.append((name, i + (n0 // 512), [(w[:, n:n + 512].rearrange("(k p) n -> p k n", p=P), 0, 8, 0, 512)]))

    def tall(name, w, n0=0):
        kc = w.shape[0] // P
        for i, k in enumerate(range(0, kc, 4)):
            n = min(4, kc - k)
            plan.append((name, i, [(w[k * P:(k + n) * P, n0:n0 + D].rearrange("(k p) n -> p k n", p=P), 0, n, 0, D)]))

    def gate_up(name, w):
        for i, n in enumerate(range(0, DFF, 256)):
            plan.append((name, i, [(w[:, n:n + 256].rearrange("(k p) n -> p k n", p=P), 0, 8, 0, 256),
                                   (w[:, DFF + n:DFF + n + 256].rearrange("(k p) n -> p k n", p=P), 0, 8, 256, 512)]))

    wide("mod", a["w_mod"][0], 0, 2048)
    for i, mods in enumerate(((4, 5), (6, 7), (8, 9), (10, 11), (), ())):
        wide("in", a["w_in"][0], 512 * i, 512 * (i + 1))
        for m in mods:
            wide("mod", a["w_mod"][0], 512 * m, 512 * (m + 1))
    tall("out", a["w_out"][0])
    wide("wq", a["peer_w_query"][0])
    for l in range(2):
        wide(f"mk{l}", a["mem_w_kv_2"][l], 0, D)
        tall(f"mv{l}", a["mem_w_kv_2"][l], D)
    wide("cin", a["conv_w_in_2"][0])
    tall("cout", a["conv_w_out_2"][0])
    for l in range(2):
        if l == 1:
            tall("bk", a["w_kv_2"], 0)
            tall("bv", a["w_kv_2"], D)
            tall("bq", a["moba_w_q_2"][0])
            tall("bo", a["moba_w_o_2"][0])
        wide(f"mq{l}", a["mem_w_q_2"][l])
        tall(f"mo{l}", a["mem_w_o_2"][l])
        gate_up(f"gu{l}", a["ffn_w_gu_2"][l])
        tall(f"dn{l}", a["ffn_w_down_2"][l])
    return plan


LINEAR = ([(f"in{c}", "DA") for c in ("0", "0c", "1", "1c")] + [("in2", "A"), ("in3", "DA")]
          + [(f"in{c}", "DA") for c in ("4", "4c", "5", "5c")] + [("g2row", "DA")]
          + [("ret", "D")] * 4 + [("diff", "DA")] * 8 + [("arow", "DA"), ("brow", "DA")]
          + [("out", "D")] * 2 + [("wq", "DA")] * 4 + [("key", "DA")] * 4 + [("g5row", "DA")]
          + [("mkv", "A")] * 8 + [("cb", "DA")] * 4 + [("cu", "D")] * 2 + [("cout", "D")] * 2)
for _l in range(2):
    if _l:
        LINEAR += [("bk", "DA")] * 2 + [("bv", "DA")] * 2 + [("bq", "DA")] * 2 + [("bs", "D")] * 8 + [("bo", "D")] * 2
    LINEAR += [(f"mq{_l}", "DA")] * 2 + [(f"ms{_l}", "DA")] * 4 + [(f"mo{_l}", "D")] * 2
    LINEAR += [(f"gu{_l}", "DA")] * 11 + [(f"dn{_l}", "D")] * 2
TURNS = ([("vec", 1), ("sk", 4), ("x", 4), ("ctx", 4), ("mem", 4), ("rq", 1), ("rkc", 1), ("rk", 1), ("dkc", 2),
          ("dq", 2), ("dk", 2), ("at", 8), ("mix", 4), ("h2", 4), ("conv", 4)]
         + [("mem0", 4), ("pm0", 4), ("ffn0", 4), ("blk", 4), ("bqT", 4), ("bkT", 4), ("pb", 8)]
         + [("mem1", 4), ("pm1", 4), ("ffn1", 4)])
OUTS = [("om0", 4), ("ob", 4), ("om1", 4)]


def freed_after(n, who):
    return sum(who in w for _, w in LINEAR[:n + 1])


def first_of(entries, name):
    return [n for n, _ in entries].index(name)


def turn(name):
    at = 0
    for n, k in TURNS:
        if n == name:
            return at
        at += k
    raise KeyError(name)


def out_use(name):
    at = 0
    for n, k in OUTS:
        if n == name:
            return at
        at += k
    raise KeyError(name)


def lin(name):
    return first_of(LINEAR, name)


def freed(n, who):
    return sum(who in w for _, w in LINEAR[:max(n - 1, 0)])


NORMS = ["x", "ctx", "mem", "h2", "conv", "mem0", "ffn0", "blk", "mem1", "ffn1", "final"]


def build_program(nc, a, out):
    plan = weight_plan(a)
    piece = {}
    for n, (name, i, _) in enumerate(plan):
        piece[name, i] = n

    with ExitStack() as ctx:
        def sb(name, cols, dt=F32):
            return ctx.enter_context(nc.sbuf_tensor(name, [P, cols], dt))

        sems = {}

        def sem(name):
            if name not in sems:
                sems[name] = ctx.enter_context(nc.semaphore(name))
            return sems[name]

        keep = sb("keep", K_END)
        ones = sb("ones", P)
        cols = sb("cols", 184)
        modc = sb("modc", 96)
        aff = sb("aff", 48)
        x_all = sb("x_all", 2048)
        hT_all = sb("hT_all", 2048)
        h2_all = sb("h2_all", 2048)
        mem_all = sb("mem_all", 8192)
        s_all = sb("s_all", 4096)
        ring = sb("ring", RING * 4096)
        arena = sb("arena", 2 * SLOTS * 1024)
        stat = sb("stat", 11 * 8)
        small = sb("small", 300)
        pidx = sb("pidx", 64, U32)
        ptop = sb("ptop", 80, U32)
        pf = sb("pf", 348)

        ident = keep[:, K_ID:K_ID + P]
        iota16 = keep[:, K_IOTA:K_IOTA + 16]
        x = x_all[:, :].rearrange("p (t d) -> p t d", t=NT)
        hT = hT_all[:, :].rearrange("p (k n) -> p k n", k=KC)
        h2 = h2_all[:, :].rearrange("p (t d) -> p t d", t=NT)
        h2T = h2_all[:, :].rearrange("p (k n) -> p k n", k=KC)
        mem = [mem_all[:, i * 2048:(i + 1) * 2048] for i in range(4)]

        def toks(v):
            return v.rearrange("p (t d) -> p t d", t=NT)

        def feat(v):
            return v.rearrange("p (k n) -> p k n", n=TOK)

        mod = modc[:, :].rearrange("p (n v) -> p n v", v=2)
        slot8 = [ring[:, i * 4096:(i + 1) * 4096].rearrange("p (k n) -> p k n", k=8) for i in range(RING)]
        slot4 = [ring[:, i * 4096:(i + 1) * 4096].rearrange("p (k n) -> p k n", k=4) for i in range(RING)]

        PR = arena[:, 0:6144].rearrange("p (t n) -> p t n", t=NT)
        PC = arena[:, 6144:9728].rearrange("p (t n) -> p t n", t=NT)
        DEC = arena[:, 9728:13824].rearrange("p (h j n) -> p h j n", h=RH, j=4)
        skT = arena[:, 13824:15872].rearrange("p (g n) -> p g n", g=16)
        sk_raw = arena[:, 0:2048].rearrange("p (g n) -> p g n", g=16)
        dist = s_all[:, 0:2048].rearrange("p (a j n) -> p a j n", a=4, j=2)
        aux = arena[:, 15872:16384]
        dtmp = arena[:, 2048:6144].rearrange("p (h s j n) -> p h s j n", h=RH, s=2, j=2)
        vec_raw = hT_all[:, 0:256]
        ctx_x, ctxT = toks(mem[0]), feat(mem[1])
        mem_x = toks(s_all[:, 2048:4096])
        memT = [feat(mem[2]), feat(mem[3])]
        tmpA, tmpB = s_all[:, 0:1024], s_all[:, 1024:2048]
        rqT = s_all[:, 2048:2560].rearrange("p (b n) -> p b n", b=2)
        rkT = s_all[:, 2560:3584].rearrange("p (b n) -> p b n", b=2)
        dqT = hT_all[:, 0:1024].rearrange("p (h n) -> p h n", h=DH)
        dkT = mem[1].rearrange("p (h n) -> p h n", h=DH)
        PT = mem[0].rearrange("p (b j n) -> p b j n", b=2, j=4)
        EX = mem[0].rearrange("p (b s n) -> p b s n", b=2, s=2)
        aT = s_all[:, 0:1024].rearrange("p (b j n) -> p b j n", b=2, j=4)
        g2row = hT_all[:, 1024:2048]
        arow, brow = mem[1][:, 0:1024], mem[1][:, 1024:2048]
        g5row = hT_all[:, 0:1024]
        qT = arena[:, 0:4096].rearrange("p (g n) -> p g n", g=16)
        SC = s_all[:, :].rearrange("p (g s n) -> p g s n", g=16, s=2)
        uslot = [arena[:, i * 1024:(i + 1) * 1024] for i in range(SLOTS)]
        vslot = [arena[:, (SLOTS + i) * 1024:(SLOTS + i + 1) * 1024] for i in range(SLOTS)]
        cand, cand2, hot = hT_all[:, 1024:1280], hT_all[:, 1280:1536], hT_all[:, 1536:1792]
        diag = [hT_all[:, 1792:1920], hT_all[:, 1920:2048]]
        bT, cT = feat(arena[:, 0:2048]), feat(arena[:, 2048:4096])
        zT = arena[:, 4096:6160].rearrange("p (k n) -> p k n", k=KC)
        cvT = feat(arena[:, 6160:8208])
        mqT, oT = feat(arena[:, 0:2048]), feat(arena[:, 2048:4096])
        pE = arena[:, 4096:5120].rearrange("p (b t n) -> p b t n", b=2, t=NT)
        pT = arena[:, 5120:6144].rearrange("p (b k n) -> p b k n", b=2, k=2)
        sg = arena[:, 0:1024].rearrange("p (b n) -> p b n", b=2)
        fT = feat(arena[:, 4096:4096 + FC * TOK])
        kvT = feat(arena[:, 0:2048])
        bqk = arena[:, 2048:6144].rearrange("p (t s n) -> p t s n", t=NT, s=2)
        bv = toks(arena[:, 6144:8192])
        bqT, bkT = feat(arena[:, 8192:10240]), feat(arena[:, 10240:12288])
        boT = feat(arena[:, 12288:14336])
        bE = s_all[:, 0:1024].rearrange("p (b t n) -> p b t n", b=2, t=NT)
        bPT = s_all[:, 1024:2048].rearrange("p (b k n) -> p b k n", b=2, k=2)
        frow = s_all[:, 2048:3072]
        rot = s_all[:, 3072:3584].rearrange("p (s g n) -> p s g n", s=2, g=16)

        at = [0]

        def sm(n):
            at[0] += n
            assert at[0] <= 300
            return small[:, at[0] - n:at[0]]

        lg, lgt = sm(8), sm(8)
        cs = sm(16)
        lam, lam2 = sm(1), sm(2)
        mx, nmx, zz, rz = sm(4), sm(4), sm(4), sm(4)
        dss, dms, dsd, drs = sm(24), sm(24), sm(24), sm(24)
        yss, yms, ysd, yrs = sm(8), sm(8), sm(8), sm(8)
        gd = sm(4)
        cosb, sinb = sm(32), sm(32)
        posf = sm(2)
        lg_raw8, lg2, lg3, lg4 = sm(8), sm(8), sm(8), sm(8)
        pos_i = pidx[:, 0:2].bitcast(I32)

        def mod_part(i):
            return h2_all[:, (i % 4) * 512:(i % 4 + 1) * 512]

        def mod_part2(i, v):
            return s_all[:, (i - 1 + v) * 512:(i + v) * 512]

        MOD_SUMS = (1, 3, 4, 5, 6, 7, 8, 9, 10, 11)

        a_x, a_c, a_2 = aff[:, 0:8], aff[:, 8:16], aff[:, 16:24]

        bank = [ctx.enter_context(nc.psum_tensor(f"bank{i}", [P, 512], F32)) for i in range(8)]
        T = [bank[4], bank[5]]
        M = [bank[6], bank[7]]

        def L(n, b):
            return bank[2 * (n % 2) + b]

        def two(b):
            return b[:, :].rearrange("p (a n) -> p a n", a=2)

        def like(src, dst):
            s = dst.shape
            return src if len(s) == 2 else src.rearrange("p (a n) -> p a n", a=s[1])

        block = ctx.enter_context(nc.Block())
        landed = [sem(f"weights_in_slot{i}") for i in range(RING)]
        u_in = [sem(f"u_row_in_slot{i}") for i in range(SLOTS)]
        v_in = [sem(f"v_row_in_slot{i}") for i in range(SLOTS)]
        piece_used = sem("piece_used")
        lin_ready, lin_free = sem("linear_ready"), {w: sem(f"linear_free_{w}") for w in "DA"}
        turn_ready, turn_free = sem("turn_ready"), [sem("turn_free_D"), sem("turn_free_A")]
        x_ready, steps = sem("x_ready"), sem("vector_steps")
        sums_ready, ms_ready, sd_ready, rs_ready = (sem(n) for n in ("sums_ready", "ms_ready", "sd_ready", "rs_ready"))
        xn_ready = [sem("xn_ready_tile0"), sem("xn_ready_tile1")]
        dots_done, v_used = sem("dots_done"), sem("v_rows_used")

        norm_at = {"x": (x, h2, h2), "ctx": (ctx_x, toks(mem[1]), ctx_x), "mem": (mem_x, toks(mem[2]), mem_x)}
        nmx_ready, probs_ready, out_ready = sem("max_ready"), sem("probs_ready"), sem("out_ready")
        out_free = [sem("out_free_D"), sem("out_free_A")]



        best4, gate4, nbest4, pz4 = pf[:, 0:64], pf[:, 64:128], pf[:, 128:132], pf[:, 132:136]
        pact2, pgel2, pw2 = pf[:, 136:168], pf[:, 168:200], pf[:, 200:232]
        top_v, top_i, top_pos, top_sel, prz = pf[:, 232:264], pf[:, 264:296], pf[:, 296:328], pf[:, 328:344], pf[:, 344:345]
        u_topi, u_pos, u_hl = ptop[:, 0:32], ptop[:, 32:48], ptop[:, 48:80]
        cur = hot

        tall_names = [n for n in dict.fromkeys(p[0] for p in plan) if n in
                      ("out", "mv0", "mv1", "cout", "mo0", "mo1", "dn0", "dn1", "bk", "bv", "bq", "bo")]
        last_piece = {n: max(i for m, i, _ in plan if m == n) for n in tall_names}
        middle = [(n, i) for n, i, _ in plan if n in tall_names and i != last_piece[n]]
        mkv = {"mk0": 0, "mv0": 2, "mk1": 4, "mv1": 6}

        def use_of(name):
            return lin("mkv") + mkv[name] if name in mkv else lin(name)

        def wait_released(eng, n):
            name, i, _ = plan[n]
            if name == "mod":
                if i in (0, 2):
                    eng.wait_ge(sem("mod_done"), i // 2 + 1)
                else:
                    eng.wait_ge(sem("mod_sums"), MOD_SUMS.index(i) + 1)
            elif name == "in":
                eng.wait_ge(lin_ready, 2 * (lin(f"in{i}c" if i in (0, 1, 4, 5) else f"in{i}") + 1))
            elif (name, i) in middle:
                eng.wait_ge(sem("piece_used"), middle.index((name, i)) + 1)
            elif name in tall_names:
                eng.wait_ge(lin_ready, 2 * (use_of(name) + 2))
            elif name == "cin":
                eng.wait_ge(lin_ready, 2 * (lin("cb") + i + 1))
            else:
                eng.wait_ge(lin_ready, 2 * (use_of(name) + i + 1))


        @block.sync
        def _(sp):
            sp.dma_start(keep[:, :], a["keep"]).then_inc(sem("consts_in"), 16)
            for name, r, c in (("c", C_C, 0), ("c_ctx", C_CC, 0), ("norm1_g", C_N1, 0), ("norm2_g", C_N2, 0),
                               ("norm_mix_2", C_MIX, 0), ("norm_mem_2", C_MEM, 0), ("norm_memkv_2", C_MKV, 0),
                               ("norm_ffn_2", C_FFN, 0), ("kv_norm_2", C_KV, 0), ("conv_w_2", C_CONV, 0),
                               ("b_mod", 0, P), ("ret_norm_g", 48, P), ("diff_norm_g", 52, P)):
                src = a[name].flatten().rearrange("(r n) -> r n", n=P)
                sp.dma_start(vec_raw[r:r + src.shape[0], c:c + P], src).then_inc(sem("vecs_in"), 16)
            for n, (name, i, parts) in enumerate(plan):
                if n == 2:
                    sp.dma_start(x, a["x"][0].rearrange("(t p) d -> p t d", p=P)).then_inc(sem("x_in"), 16)
                    sp.dma_start(ctx_x, a["ctx"][0].rearrange("(t p) d -> p t d", p=P)).then_inc(sem("ctx_in"), 16)
                if n >= RING:
                    wait_released(sp, n - RING)
                for src, k0, k1, c0, c1 in parts:
                    dst = (slot4 if c1 == D else slot8)[n % RING][:, k0:k1, c0:c1]
                    sp.dma_start(dst, src).then_inc(landed[n % RING], 32 // len(parts))
            for t in range(NT):
                sp.wait_ge(sem("y_done"), t + 1)
                sp.dma_start(out[0].rearrange("(t p) d -> p t d", p=P)[:, t], h2[:, t]).then_inc(sem("stored"), 16)
            sp.wait_ge(sem("stored"), 32)

        @block.tensor
        def _(pe):
            mm, tr = nc.tensor.matmul, nc.tensor.transpose

            def weights(n, i=0):
                pe.wait_ge(landed[n % RING], 32 * (n // RING + 1) + 32 * i)
                return n % RING

            def lin_open(n, i=0):
                for w in "DA":
                    if freed(n, w):
                        pe.wait_ge(lin_free[w], freed(n, w) + 4 * i)

            def lin_read(n):
                for w in LINEAR[n][1]:
                    pe.wait_ge(lin_free[w], freed_after(n, w))

            def turn_open(n):
                if n >= 2:
                    pe.wait_ge(turn_free[n % 2], n // 2)

            def turned(n):
                pe.wait_ge(turn_free[n % 2], n // 2 + 1)

            def wait_acts(name):
                turned(turn(name) + 2)
                turned(turn(name) + 3)

            def turn_tokens(name, src):
                if name in NORMS:
                    pe.wait_ge(xn_ready[0], NORMS.index(name) + 1)
                    pe.wait_ge(xn_ready[1], NORMS.index(name) + 1)
                for u in range(4):
                    n = turn(name) + u
                    turn_open(n)
                    for cc in range(2):
                        for t in range(NT):
                            i = tr(T[n % 2][:, (2 * cc + t) * P:(2 * cc + t + 1) * P], src(t, 2 * u + cc), ident)
                    i.then_inc(turn_ready, 1)

            def features_out(n, p, src, i=0):
                w = weights(p, i)
                lin_open(n, i)
                for b in range(4):
                    for k in range(KC):
                        m = mm(L(n, b // 2)[:, (b % 2) * TOK:(b % 2 + 1) * TOK], slot8[w][:, k, b * P:(b + 1) * P],
                               src[:, k], start=(k == 0), stop=(k == KC - 1))
                    if b % 2:
                        m.then_inc(lin_ready, 1)

            def tokens_out(n, name, src, kc=KC, wait_k=None):
                lin_open(n)
                lin_open(n + 1)
                for k in range(kc):
                    if wait_k:
                        wait_k(k)
                    if k % 4 == 0:
                        w = weights(piece[name, k // 4])
                    for half in range(2):
                        for t in range(NT):
                            m = mm(L(n + half, t)[:, :], src[:, k, t * P:(t + 1) * P],
                                   slot4[w][:, k % 4, half * 512:(half + 1) * 512], start=(k == 0), stop=(k == kc - 1))
                            if k == kc - 1:
                                m.then_inc(lin_ready, 1)
                    if k % 4 == 3 and k != kc - 1:
                        m.then_inc(sem("piece_used"), 1)

            def row(n, name, k):
                pe.wait_ge(sem("rows_diag"), k)
                lin_open(n)
                for b in range(2):
                    mm(L(n, b)[:, :], ones[:, :], name[:, b * 512:(b + 1) * 512], start=True, stop=True).then_inc(lin_ready, 1)

            pe.wait_ge(sem("consts_in"), 16)
            pe.wait_ge(sem("vecs_in"), 16 * 13)
            tr(T[0][:, 0:P], vec_raw[:, 0:P], ident)
            tr(T[0][:, P:P + 56], vec_raw[0:56, P:2 * P], keep[0:56, 0:56]).then_inc(turn_ready, 1)
            pe.wait_ge(sem("keys_in"), 16)
            for u in range(4):
                n = turn("sk") + u
                turn_open(n)
                for j in range(4):
                    i = tr(T[n % 2][:, j * P:(j + 1) * P], sk_raw[:, 4 * u + j], ident)
                i.then_inc(turn_ready, 1)

            csil = cs.rearrange("p (v k) -> p k v", v=2)

            def modulation(i):
                w = weights(piece["mod", i])
                for b in range(4):
                    for k in range(KC):
                        m = mm(M[1][:, 8 * i + 2 * b:8 * i + 2 * b + 2], slot8[w][:, k, b * P:(b + 1) * P], csil[:, k],
                               start=(k == 0), stop=(k == KC - 1))
                m.then_inc(sem("mod_done"), 1)

            def modulation_columns(i):
                pe.wait_ge(sem("mod_sums"), MOD_SUMS.index(i) + 1)
                for b in range(4):
                    if i < 4:
                        for v in range(2):
                            c = 8 * i + 2 * b + v
                            m = mm(M[1][:, c:c + 1], mod_part2(i, v)[:, b * P:(b + 1) * P], ones[:, 0:1], start=True, stop=True)
                        continue
                    m = mm(M[1][:, 8 * i + 2 * b:8 * i + 2 * b + 2], mod_part(i)[:, b * P:(b + 1) * P], ones[:, 0:2], start=True, stop=True)
                m.then_inc(sem("mod_done"), 1)

            pe.wait_ge(sem("c_silu"), 1)
            modulation(0)
            modulation(2)
            modulation_columns(1)
            modulation_columns(3)
            turn_tokens("x", lambda t, c: h2[:, t, c * P:(c + 1) * P])
            turn_tokens("ctx", lambda t, c: ctx_x[:, t, c * P:(c + 1) * P])
            turn_tokens("mem", lambda t, c: mem_x[:, t, c * P:(c + 1) * P])
            for c in range(6):
                if c == 0:
                    wait_acts("x")
                w = weights(piece["in", c])
                for side, src in (("", hT), ("c", ctxT)):
                    if side and c in (2, 3):
                        continue
                    if side and c == 0:
                        wait_acts("ctx")
                    n = lin(f"in{c}{side}")
                    lin_open(n)
                    c0 = 256 if side and c == 0 else 0
                    for t in range(NT):
                        for k in range(KC):
                            m = mm(L(n, t)[:, 0:512 - c0], src[:, k, t * P:(t + 1) * P], slot8[w][:, k, c0:512],
                                   start=(k == 0), stop=(k == KC - 1))
                        m.then_inc(lin_ready, 1)
                for i in {1: (4, 5), 2: (6, 7), 3: (8, 9), 5: (10, 11)}.get(c, ()):
                    modulation_columns(i)
            row(lin("g2row"), g2row, 1)
            pe.wait_ge(sem("roped"), 2)
            n = turn("rq")
            turn_open(n)
            for b in range(2):
                for t in range(NT):
                    i = tr(T[n % 2][:, (2 * b + t) * P:(2 * b + t + 1) * P], PR[:, t, b * P:(b + 1) * P], ident)
            i.then_inc(turn_ready, 1)
            n = turn("rkc")
            lin_read(lin("in0c"))
            turn_open(n)
            for b in range(2):
                for t in range(NT):
                    i = tr(T[n % 2][:, (2 * b + t) * P:(2 * b + t + 1) * P], PC[:, t, b * P:(b + 1) * P], ident)
            i.then_inc(turn_ready, 1)
            n = turn("rk")
            turn_open(n)
            for b in range(2):
                for t in range(NT):
                    i = tr(T[n % 2][:, (2 * b + t) * P:(2 * b + t + 1) * P], PR[:, t, 256 + b * P:256 + (b + 1) * P], ident)
            i.then_inc(turn_ready, 1)
            for name, src, c0, k in (("dkc", PC, 768, 4), ("dq", PR, 1536, 6), ("dk", PR, 2048, 6)):
                pe.wait_ge(sem("roped"), k)
                for u in range(2):
                    n = turn(name) + u
                    turn_open(n)
                    for hh in range(2):
                        for t in range(NT):
                            h = 2 * u + hh
                            i = tr(T[n % 2][:, (2 * hh + t) * P:(2 * hh + t + 1) * P], src[:, t, c0 + h * P:c0 + (h + 1) * P], ident)
                    i.then_inc(turn_ready, 1)

            def ret_scores(h):
                n = lin("ret") + h
                lin_open(n)
                s = slice(64 * (h % 2), 64 * (h % 2) + 64)
                for j in range(4):
                    m = mm(L(n, j // 2)[:, (j % 2) * TOK:(j % 2 + 1) * TOK], rkT[s, h // 2, j * P:(j + 1) * P], rqT[s, h // 2, :],
                           start=True, stop=True)
                    if j % 2:
                        m.then_inc(lin_ready, 1)

            def ret_out(h):
                lin_read(lin("ret") + h)
                for t in range(NT):
                    for j in range(4):
                        v = PC[:, j, 256 + h * P:256 + (h + 1) * P] if j < 2 else PR[:, j - 2, 512 + h * P:512 + (h + 1) * P]
                        m = mm(M[t][:, h * P:(h + 1) * P], PT[:, h % 2, j, t * P:(t + 1) * P], v, start=(j == 0), stop=(j == 3))
                m.then_inc(sem("ret_out"), 1)

            turned(turn("rk"))
            turned(turn("rkc"))
            turned(turn("rq"))
            pe.wait_ge(sem("mod_cols"), 2)
            lin_read(lin("in5c"))
            ret_scores(0)
            for h in range(RH):
                if h + 1 < RH:
                    ret_scores(h + 1)
                ret_out(h)

            def diff_scores(i):
                h, t, n = i // 2, i % 2, lin("diff") + i
                lin_open(n)
                for p in range(2):
                    s = slice(64 * p, 64 * p + 64)
                    mm(L(n, p)[:, :], dqT[s, h, t * P:(t + 1) * P], dkT[s, h, :], start=True, stop=True).then_inc(lin_ready, 1)

            for m in range(turn("dkc"), turn("at")):
                if m >= turn("at") - 2:
                    turned(m)
            diff_scores(0)
            diff_scores(1)
            for i in range(8):
                h, t, n = i // 2, i % 2, turn("at") + i
                pe.wait_ge(probs_ready, i + 1)
                turn_open(n)
                for j in range(4):
                    q = tr(T[n % 2][:, j * P:(j + 1) * P], EX[:, i % 2, 0, j * P:(j + 1) * P], ident)
                q.then_inc(turn_ready, 1)
                if i + 2 < 8:
                    diff_scores(i + 2)
                if i == 0:
                    pe.wait_ge(sem("mix_D"), 1)
                turned(n)
                for j in range(4):
                    v = PC[:, j, 1280 + h * P:1280 + (h + 1) * P] if j < 2 else PR[:, j - 2, 2560 + h * P:2560 + (h + 1) * P]
                    m = mm(M[t][:, h * P:(h + 1) * P], aT[:, i % 2, j], v, start=(j == 0), stop=(j == 3))
                m.then_inc(sem("diff_out"), 1)
            row(lin("arow"), arow, 2)
            row(lin("brow"), brow, 3)
            pe.wait_ge(sem("mix_D"), 2)
            pe.wait_ge(sem("mix_A"), 1)
            turn_tokens("mix", lambda t, c: PR[:, t, c * P:(c + 1) * P] if c < 4 else PR[:, t, 1536 + (c - 4) * P:1536 + (c - 3) * P])
            wait_acts("mix")
            tokens_out(lin("out"), "out", h2T)
            turn_tokens("h2", lambda t, c: h2[:, t, c * P:(c + 1) * P])
            wait_acts("h2")
            for c in range(4):
                features_out(lin("wq") + c, piece["wq", c], hT)
            for c in (2, 3):
                lin_read(lin("wq") + c)
            for t in range(NT):
                for half in range(2):
                    n = lin("key") + 2 * t + half
                    lin_open(n)
                    for j in range(8):
                        g = half * 8 + j
                        m = mm(L(n, j // 4)[:, (j % 4) * P:(j % 4 + 1) * P], qT[:, g, t * P:(t + 1) * P], skT[:, g],
                               start=True, stop=True)
                        if j % 4 == 3:
                            m.then_inc(lin_ready, 1)
            row(lin("g5row"), g5row, 4)

            def memory_kv(name):
                l = int(name[2])
                if name[1] == "k":
                    for i in range(2):
                        yield lambda i=i: features_out(lin("mkv") + mkv[name] + i, piece[name, i], memT[l])
                else:
                    yield lambda: tokens_out(lin("mkv") + mkv[name], name, memT[l])

            wait_acts("mem")
            insert = {0: [], 2: [], 4: [], 8: [], 10: [], 12: []}
            for l in range(2):
                k0, k1 = memory_kv(f"mk{l}")
                insert[8 * l].append(k0)
                insert[8 * l + 2].append(k1)
                insert[8 * l + 4] += list(memory_kv(f"mv{l}"))
            for g in range(16):
                for f in insert.get(g, ()):
                    f()
                acc = M if g < 8 else T
                for k in range(PK):
                    n = 16 * g + k
                    pe.wait_ge(sem("diag_ready"), n + 1)
                    pe.wait_ge(v_in[k % SLOTS], 16 * (2 * g + k // SLOTS + 1))
                    for b in range(2):
                        m = mm(acc[b][:, :], diag[k % 2], vslot[k % SLOTS][:, b * 512:(b + 1) * 512],
                               start=(n % 128 == 0), stop=(n % 128 == 127))
                    m.then_inc(v_used, 1)

            turn_tokens("conv", lambda t, c: h2[:, t, c * P:(c + 1) * P])
            wait_acts("conv")
            for c in range(6):
                features_out(lin("cb") + c, piece["cin", c], hT)
            tokens_out(lin("cout"), "cout", cvT, wait_k=lambda k: pe.wait_ge(sem("conv_done"), k // 4 + 1) if k % 4 == 0 else None)

            def memory_attention(l):
                turn_tokens(f"mem{l}", lambda t, c: h2[:, t, c * P:(c + 1) * P])
                wait_acts(f"mem{l}")
                for c in range(2):
                    features_out(lin(f"mq{l}") + c, piece[f"mq{l}", c], hT)
                K, V = feat(mem[2 * l]), toks(mem[2 * l + 1])

                def scores(h):
                    n = lin(f"ms{l}") + h
                    lin_open(n)
                    for t in range(NT):
                        for e in range(2):
                            m = mm(L(n, t)[:, 0:TOK], mqT[:, 2 * h + e, t * P:(t + 1) * P], K[:, 2 * h + e],
                                   start=(e == 0), stop=(e == 1))
                        m.then_inc(lin_ready, 1)

                for c in range(2):
                    lin_read(lin(f"mq{l}") + c)
                scores(0)
                scores(1)
                p0 = 8 if l == 0 else 20
                for h in range(MH):
                    n, o = turn(f"pm{l}") + h, out_use(f"om{l}") + h
                    pe.wait_ge(probs_ready, p0 + h + 1)
                    turn_open(n)
                    for k in range(2):
                        for t in range(NT):
                            i = tr(T[n % 2][:, (2 * k + t) * P:(2 * k + t + 1) * P], pE[:, h % 2, t, k * P:(k + 1) * P], ident)
                    i.then_inc(turn_ready, 1)
                    if h + 2 < MH:
                        scores(h + 2)
                    turned(n)
                    if o >= 2:
                        pe.wait_ge(out_free[o % 2], o // 2)
                    for e in range(2):
                        for k in range(2):
                            m = mm(M[o % 2][:, e * TOK:(e + 1) * TOK], V[:, k, (2 * h + e) * P:(2 * h + e + 1) * P], pT[:, h % 2, k],
                                   start=(k == 0), stop=(k == 1))
                    m.then_inc(out_ready, 1)
                for o in (out_use(f"om{l}") + 2, out_use(f"om{l}") + 3):
                    pe.wait_ge(out_free[o % 2], o // 2 + 1)
                tokens_out(lin(f"mo{l}"), f"mo{l}", oT)

            def feed_forward(l):
                turn_tokens(f"ffn{l}", lambda t, c: h2[:, t, c * P:(c + 1) * P])
                wait_acts(f"ffn{l}")
                n0, p0 = lin(f"gu{l}"), piece[f"gu{l}", 0]
                with pe.Fori(0, 2) as i:
                    for j in range(4):
                        features_out(n0 + j, p0 + j, hT, i)
                for j in range(8, 11):
                    features_out(n0 + j, p0 + j, hT)
                tokens_out(lin(f"dn{l}"), f"dn{l}", fT, FC,
                           lambda k: pe.wait_ge(lin_free["D"], freed_after(n0 + k // 2, "D")) if k % 2 == 0 else None)

            memory_attention(0)
            feed_forward(0)
            turn_tokens("blk", lambda t, c: h2[:, t, c * P:(c + 1) * P])
            wait_acts("blk")
            tokens_out(lin("bk"), "bk", kvT)
            tokens_out(lin("bv"), "bv", kvT)
            tokens_out(lin("bq"), "bq", hT)
            pe.wait_ge(sem("brot"), 2)
            turn_tokens("bqT", lambda t, c: bqk[:, t, 0, c * P:(c + 1) * P])
            turn_tokens("bkT", lambda t, c: bqk[:, t, 1, c * P:(c + 1) * P])
            lin_read(lin("bv") + 1)

            def block_scores(h):
                n = lin("bs") + h
                lin_open(n)
                mm(L(n, 0)[:, 0:P], bqT[:, h, 0:P], bkT[:, h, 0:P], start=True, stop=True).then_inc(lin_ready, 1)
                mm(L(n, 1)[:, 0:TOK], bqT[:, h, P:TOK], bkT[:, h, :], start=True, stop=True).then_inc(lin_ready, 1)

            turned(turn("bkT") + 2)
            turned(turn("bkT") + 3)
            block_scores(0)
            block_scores(1)
            for h in range(BH):
                n, o = turn("pb") + h, out_use("ob") + h // 2
                pe.wait_ge(probs_ready, 12 + h + 1)
                turn_open(n)
                tr(T[n % 2][:, 0:P], bE[:, h % 2, 0, 0:P], ident)
                tr(T[n % 2][:, P:2 * P], bE[:, h % 2, 1, 0:P], ident)
                tr(T[n % 2][:, 2 * P:3 * P], bE[:, h % 2, 1, P:2 * P], ident).then_inc(turn_ready, 1)
                if h + 2 < BH:
                    block_scores(h + 2)
                turned(n)
                if h % 2 == 0:
                    pe.wait_ge(out_free[o % 2], o // 2)
                c0 = (h % 2) * TOK
                pv = bPT[:, h % 2].rearrange("p k n -> p (k n)")
                mm(M[o % 2][:, c0:c0 + TOK], bv[:, 0, h * P:(h + 1) * P], pv[:, 0:TOK], start=True, stop=False)
                mm(M[o % 2][:, c0 + P:c0 + TOK], bv[:, 1, h * P:(h + 1) * P], pv[:, TOK:TOK + P], start=False, stop=True).then_inc(out_ready, 1)
            for o in (out_use("ob") + 2, out_use("ob") + 3):
                pe.wait_ge(out_free[o % 2], o // 2 + 1)
            tokens_out(lin("bo"), "bo", boT)
            memory_attention(1)
            feed_forward(1)

        def out_need(o):
            ob = out_use("ob")
            return o + 1 if o < ob else (ob + 2 * (o - ob + 1) if o < ob + 4 else o + 5)

        def norm_wait(eng, name):
            if name in ("x", "ctx", "mem"):
                eng.wait_ge(sem(name + "_in"), 16)
            elif name in ("h2", "conv"):
                eng.wait_ge(x_ready, 4 if name == "h2" else 8)
            else:
                last = {"mem0": "cout", "ffn0": "mo0", "blk": "dn0", "mem1": "bo", "ffn1": "mo1", "final": "dn1"}[name]
                eng.wait_ge(lin_free["D"], freed_after(lin(last) + 1, "D"))

        def stats(name):
            k = NORMS.index(name)
            return k, stat[:, 8 * k:8 * k + 2], stat[:, 8 * k + 2:8 * k + 4], stat[:, 8 * k + 4:8 * k + 6], stat[:, 8 * k + 6:8 * k + 8]

        def places(name):
            return norm_at.get(name, (x, h2, h2))

        def scaled(name):
            if name == "x":
                return [(hT, lambda c: a_x[:, c:c + 1], lambda c: mod[:, c, 0:1])]
            if name == "ctx":
                return [(ctxT, lambda c: a_c[:, c:c + 1], lambda c: mod[:, c, 1:2])]
            if name == "mem":
                return [(memT[l], lambda c, l=l: cols[:, C_MKV + 8 * l + c:C_MKV + 8 * l + c + 1], None) for l in range(2)]
            if name == "mix":
                return [(h2T, lambda c: cols[:, C_RN + c:C_RN + c + 1] if c < 4 else gd[:, c - 4:c - 3], None)]
            if name == "h2":
                return [(hT, None, None)]
            if name == "blk":
                return [(kvT, lambda c: cols[:, C_KV + c:C_KV + c + 1], None),
                        (hT, lambda c: cols[:, C_MIX + 8 + c:C_MIX + 8 + c + 1], None)]
            c0 = {"conv": C_MIX, "mem0": C_MEM, "mem1": C_MEM + 8, "ffn0": C_FFN, "ffn1": C_FFN + 8}[name]
            return [(hT, lambda c: cols[:, c0 + c:c0 + c + 1], None)]

        MSCALE, BSCALE, DSCALE = (D // MH) ** -0.5, (D // BH) ** -0.5, DD ** -0.5

        @block.scalar
        def _(act):
            f = nc.scalar.activation
            act.dma_start(s_all[:, 0:2048], a["dist"]).then_inc(sem("dist_in"), 16)
            act.dma_start(lg_raw8, a["ret_decay_logit"].flatten().partition_broadcast(P)).then_inc(sem("lg_in"), 16)
            act.dma_start(sk_raw, a["peer_sub_keys"][0].rearrange("h s n c -> n (h s) c")).then_inc(sem("keys_in"), 16)
            act.dma_start(mem_x, a["mem_2"][0].rearrange("(t p) d -> p t d", p=P)).then_inc(sem("mem_in"), 16)
            act.dma_start(aux[:, 0:256], a["diff_lambda"].flatten().partition_broadcast(P)).then_inc(sem("lam_in"), 16)
            act.dma_start(aux[:, 256:384], a["diff_qk_norm_g"].flatten().partition_broadcast(P)).then_inc(sem("lam_in"), 16)

            def turn_copy(n, dst, wait=None):
                act.wait_ge(turn_ready, n + 1)
                if wait:
                    act.wait_ge(*wait)
                f(dst, like(T[1][:, :], dst), ACT.Copy).then_inc(turn_free[1], 1)

            def norm(name, apply=True):
                k, ss, ms, sd, rs = stats(name)
                src, junk, dst = places(name)
                norm_wait(act, name)
                for t in range(NT):
                    f(junk[:, t], src[:, t], ACT.Square, accum_out=ss[:, t:t + 1]).then_inc(sums_ready, 1)
                act.wait_ge(ms_ready, k + 1)
                f(sd, ms, ACT.Sqrt).then_inc(sd_ready, 1)
                if apply:
                    act.wait_ge(rs_ready, k + 1)
                    f(dst[:, 1], src[:, 1], ACT.Copy, scale=rs[:, 1:2]).then_inc(xn_ready[1], 1)

            def turn_scaled(name):
                for u in (1, 3) if turn(name) % 2 == 0 else (0, 2):
                    n = turn(name) + u
                    act.wait_ge(turn_ready, n + 1)
                    dests = scaled(name)
                    for d, (dst, sc, sh) in enumerate(dests):
                        for cc in range(2):
                            c = 2 * u + cc
                            src = T[1][:, cc * TOK:(cc + 1) * TOK]
                            if sc is None:
                                q = f(dst[:, c], src, ACT.Copy)
                            elif sh is None:
                                q = f(dst[:, c], src, ACT.Copy, scale=sc(c))
                            else:
                                q = f(dst[:, c], src, ACT.Identity, scale=sc(c), bias=sh(c))
                            if cc == 1 and d == len(dests) - 1:
                                q.then_inc(turn_free[1], 1)

            act.wait_ge(turn_free[0], 1)
            f(cs, cols[:, 0:16], ACT.Silu).then_inc(sem("c_silu"), 1)
            act.wait_ge(sem("lg_abs"), 1)
            f(lgt, lgt, ACT.Exp, scale=-1.0).then_inc(sem("lg_exp"), 1)
            act.wait_ge(sem("lg_one"), 1)
            f(lg2, lg2, ACT.Ln).then_inc(sem("lg_ln"), 1)
            act.wait_ge(sem("lam_sums"), 1)
            f(lam2, lam2, ACT.Exp).then_inc(sem("lam_exp"), 1)
            act.wait_ge(sem("angles"), 1)
            f(sinb, sinb, ACT.Sin).then_inc(sem("sines"), 1)
            f(cosb, cosb, ACT.Sin).then_inc(sem("sines"), 1)
            for u in range(4):
                n = turn("sk") + u
                if n % 2:
                    turn_copy(n, skT[:, 4 * u:4 * u + 4])
            act.wait_ge(sem("dist_in"), 16)
            act.wait_ge(sem("lg_done"), 1)
            for h in range(RH):
                f(DEC[:, h, 0:2], dist[:, 0], ACT.Exp, scale=lg[:, h:h + 1]).then_inc(sem("decay_A"), 1)
                f(dtmp[:, h, 0], dist[:, 1], ACT.Exp, scale=lg[:, 4 + h:5 + h]).then_inc(sem("decay_A"), 1)
                act.wait_ge(sem("decay_arg"), h + 1)
                f(DEC[:, h, 2:4], dtmp[:, h, 1], ACT.Exp).then_inc(sem("decay_A"), 1)
            norm("x")
            norm("ctx")
            norm("mem")
            act.wait_ge(sem("mod_cols"), 1)
            turn_scaled("x")
            turn_scaled("ctx")
            turn_scaled("mem")
            for name, dst in (("in0", (PR, 0, 512)), ("in0c", (PC, 0, 256)), ("in1", (PR, 512, 512)), ("in1c", (PC, 256, 512)),
                              ("in2", None), ("in3", (PR, 1536, 512)), ("in4", (PR, 2048, 512)), ("in4c", (PC, 768, 512)),
                              ("in5", (PR, 2560, 512)), ("in5c", (PC, 1280, 512))):
                n = lin(name)
                if name == "in2":
                    act.wait_ge(lin_ready, 2 * n + 1)
                    f(PR[:, 0, 1024:1536], L(n, 0)[:, :], ACT.Silu)
                    act.wait_ge(lin_ready, 2 * n + 2)
                    f(PR[:, 1, 1024:1536], L(n, 1)[:, :], ACT.Silu).then_inc(lin_free["A"], 1)
                    continue
                buf, c, w = dst
                act.wait_ge(lin_ready, 2 * n + 2)
                f(buf[:, 1, c:c + w], L(n, 1)[:, 0:w], ACT.Copy).then_inc(lin_free["A"], 1)
                if name == "in4c":
                    for i in range(4):
                        act.wait_ge(sem("dms_ready"), i + 1)
                        c, w = ((0, 8), (8, 8), (0, 16), (0, 16))[i]
                        f(dsd[:, c:c + w], dms[:, c:c + w], ACT.Sqrt).then_inc(sem("dsd_ready"), 1)

            def row_half(n, dst):
                act.wait_ge(lin_ready, 2 * n + 2)
                f(dst[:, 512:1024], L(n, 1)[:, :], ACT.Copy).then_inc(lin_free["A"], 1)

            row_half(lin("g2row"), g2row)
            for name in ("rq", "rkc", "rk"):
                if turn(name) % 2:
                    dst = {"rq": rqT, "rkc": rkT[:, :, 0:TOK], "rk": rkT[:, :, TOK:2 * TOK]}[name]
                    turn_copy(turn(name), dst)
            for name, dst, c0 in (("dkc", dkT, 0), ("dq", dqT, 0), ("dk", dkT, TOK)):
                for u in range(2):
                    if (turn(name) + u) % 2:
                        turn_copy(turn(name) + u, dst[:, 2 * u:2 * u + 2, c0:c0 + TOK])

            def out_sums(k):
                for t in range(NT):
                    for h in range(4):
                        q = f(tmpB[:, (4 * t + h) * P:(4 * t + h + 1) * P], M[t][:, h * P:(h + 1) * P], ACT.Square, accum_out=yss[:, 4 * t + h:4 * t + h + 1])
                q.then_inc(sem("ysum"), 1)
                act.wait_ge(sem("yms"), k)
                f(ysd, yms, ACT.Sqrt).then_inc(sem("ysd"), 1)

            act.wait_ge(sem("ret_out"), RH)
            out_sums(1)
            for i in range(9):
                if i < 8:
                    n, b = lin("diff") + i, i % 2
                    act.wait_ge(nmx_ready, i + 1)
                    if i >= 2:
                        act.wait_ge(turn_ready, turn("at") + i - 1)
                    for p in range(2):
                        q = f(EX[:, b, p], L(n, p)[:, :], ACT.Exp, bias=nmx[:, 2 * b + p:2 * b + p + 1], scale=DSCALE,
                              accum_out=zz[:, 2 * b + p:2 * b + p + 1])
                    q.then_inc(lin_free["A"], 1)
                if i >= 1 and (turn("at") + i - 1) % 2:
                    j = i - 1
                    turn_copy(turn("at") + j, aT[:, j % 2], (sem("diff_out"), j - 1) if j >= 2 else None)
            act.wait_ge(sem("diff_out"), 8)
            out_sums(2)
            act.wait_ge(sem("yrs"), 2)
            for h in range(4):
                q = f(PR[:, 1, 1536 + h * P:1536 + (h + 1) * P], M[1][:, h * P:(h + 1) * P], ACT.Copy, scale=yrs[:, 4 + h:5 + h])
            q.then_inc(sem("mix_A"), 1)
            row_half(lin("arow"), arow)
            row_half(lin("brow"), brow)
            turn_scaled("mix")
            norm("h2", apply=False)
            turn_scaled("h2")
            for c in range(4):
                n = lin("wq") + c
                act.wait_ge(lin_ready, 2 * n + 2)
                f(qT[:, 4 * c + 2:4 * c + 4], two(L(n, 1)), ACT.Copy).then_inc(lin_free["A"], 1)
            for u in range(4):
                n = lin("key") + u
                act.wait_ge(lin_ready, 2 * n + 2)
                f(s_all[:, u * 1024 + 512:u * 1024 + 1024], L(n, 1)[:, :], ACT.Copy).then_inc(lin_free["A"], 1)
            row_half(lin("g5row"), g5row)

            def gate_exp(g):
                b = g % 4
                act.wait_ge(sem("topk_done"), g + 1)
                f(gate4[:, 16 * b:16 * b + 16], best4[:, 16 * b:16 * b + 16], ACT.Exp, bias=nbest4[:, b:b + 1],
                  accum_out=pz4[:, b:b + 1]).then_inc(sem("gate_exp"), 1)

            def memory_copy(l, w):
                for i in w:
                    n = lin("mkv") + 4 * l + i
                    for b in range(2):
                        act.wait_ge(lin_ready, 2 * n + b + 1)
                        dst = feat(mem[2 * l])[:, 4 * i + 2 * b:4 * i + 2 * b + 2] if i < 2 else toks(mem[2 * l + 1])[:, b, (i - 2) * 512:(i - 1) * 512]
                        q = f(dst, like(L(n, b)[:, :], dst), ACT.Copy)
                    q.then_inc(lin_free["A"], 1)

            copies = {0: (0, [0]), 2: (0, [1]), 4: (0, [2, 3]), 8: (1, [0]), 10: (1, [1]), 12: (1, [2, 3])}
            gate_exp(0)
            gate_exp(1)
            for g in range(16):
                b = g % 2
                act.wait_ge(dots_done, 16 * (g + 1))
                f(pgel2[:, 16 * b:16 * b + 16], pact2[:, 16 * b:16 * b + 16], ACT.Gelu).then_inc(sem("gelu_done"), 1)
                if g + 2 < 16:
                    gate_exp(g + 2)
                act.wait_ge(sem("weights_ready"), g + 1)
                for k in range(PK):
                    n = 16 * g + k
                    if n >= 2:
                        act.wait_ge(v_used, n - 1)
                    f(diag[k % 2], ident, ACT.Copy, scale=pw2[:, 16 * b + k:16 * b + k + 1]).then_inc(sem("diag_ready"), 1)
                    if k == 1 and g in copies:
                        memory_copy(*copies[g])
            act.wait_ge(x_ready, 8)
            act.dma_start(frow, a["norm_final_2"].partition_broadcast(P)).then_inc(sem("frow_in"), 16)
            norm("conv")
            turn_scaled("conv")
            for c in range(4):
                n = lin("cb") + c
                act.wait_ge(lin_ready, 2 * n + 2)
                dst = (bT if c < 2 else cT)[:, 4 * (c % 2) + 2:4 * (c % 2) + 4]
                f(dst, two(L(n, 1)), ACT.Copy).then_inc(lin_free["A"], 1)
            for c in range(KC):
                act.wait_ge(lin_free["D"], freed_after(lin("cu") + c // 4, "D"))
                f(cvT[:, c], zT[:, c, 0:TOK], ACT.Copy, scale=cols[:, C_CONV + c:C_CONV + c + 1]).then_inc(sem("tap0"), 1)

            def memory_attention(l):
                norm(f"mem{l}")
                turn_scaled(f"mem{l}")
                for c in range(2):
                    n = lin(f"mq{l}") + c
                    act.wait_ge(lin_ready, 2 * n + 2)
                    f(mqT[:, 4 * c + 2:4 * c + 4], two(L(n, 1)), ACT.Copy).then_inc(lin_free["A"], 1)
                m0 = 8 if l == 0 else 20
                for i in range(MH + 2):
                    if i < MH:
                        n, b = lin(f"ms{l}") + i, i % 2
                        act.wait_ge(nmx_ready, m0 + i + 1)
                        if i >= 2:
                            act.wait_ge(turn_ready, turn(f"pm{l}") + i - 1)
                        for t in range(NT):
                            q = f(pE[:, b, t], L(n, t)[:, 0:TOK], ACT.Exp, bias=nmx[:, 2 * b + t:2 * b + t + 1], scale=MSCALE,
                                  accum_out=zz[:, 2 * b + t:2 * b + t + 1])
                        q.then_inc(lin_free["A"], 1)
                    o = out_use(f"om{l}") + i
                    if 1 <= i <= MH and (turn(f"pm{l}") + i - 1) % 2:
                        turn_copy(turn(f"pm{l}") + i - 1, pT[:, (i - 1) % 2], (out_ready, out_need(o - 3)) if i >= 3 else None)
                    if i >= 2 and (o - 2) % 2:
                        act.wait_ge(out_ready, out_need(o - 2))
                        f(oT[:, 2 * (i - 2):2 * (i - 2) + 2], two(M[1]), ACT.Copy).then_inc(out_free[1], 1)

            def feed_forward(l):
                norm(f"ffn{l}")
                turn_scaled(f"ffn{l}")
                n0 = lin(f"gu{l}")

                def gate(j, i=0):
                    n = n0 + j
                    act.wait_ge(lin_ready, 2 * n + 1 + 8 * i)
                    act.wait_ge(lin_free["D"], freed_after(n - 2, "D") + 4 * i)
                    f(sg[:, j % 2], L(n, 0)[:, :], ACT.Silu).then_inc(lin_free["A"], 1)

                with act.Fori(0, 2) as i:
                    for j in range(4):
                        gate(j, i)
                for j in range(8, 11):
                    gate(j)

            memory_attention(0)
            feed_forward(0)
            norm("blk")
            turn_scaled("blk")
            for name, dst in (("bk", bqk[:, 1, 1]), ("bv", bv[:, 1]), ("bq", bqk[:, 1, 0])):
                for half in range(2):
                    n = lin(name) + half
                    act.wait_ge(lin_ready, 2 * n + 2)
                    f(dst[:, half * 512:(half + 1) * 512], L(n, 1)[:, :], ACT.Copy).then_inc(lin_free["A"], 1)
            for name, dst in (("bqT", bqT), ("bkT", bkT)):
                for u in range(4):
                    if (turn(name) + u) % 2:
                        turn_copy(turn(name) + u, dst[:, 2 * u:2 * u + 2])
            for i in range(BH + 2):
                if i < BH:
                    b = i % 2
                    act.wait_ge(nmx_ready, 12 + i + 1)
                    f(bE[:, b, 0, 0:P], bE[:, b, 0, 0:P], ACT.Exp, bias=nmx[:, 2 * b:2 * b + 1], accum_out=zz[:, 2 * b:2 * b + 1])
                    f(bE[:, b, 1], bE[:, b, 1], ACT.Exp, bias=nmx[:, 2 * b + 1:2 * b + 2],
                      accum_out=zz[:, 2 * b + 1:2 * b + 2]).then_inc(sem("bexp"), 1)
                if 1 <= i <= BH and (turn("pb") + i - 1) % 2:
                    n = turn("pb") + i - 1
                    act.wait_ge(turn_ready, n + 1)
                    if i >= 3:
                        act.wait_ge(out_ready, MH + i - 2)
                    f(bPT[:, (i - 1) % 2].rearrange("p k n -> p (k n)")[:, 0:3 * P], T[1][:, 0:3 * P], ACT.Copy).then_inc(turn_free[1], 1)
                if i >= 2 and i % 2 == 1:
                    o = out_use("ob") + (i - 2) // 2
                    if o % 2:
                        act.wait_ge(out_ready, out_need(o))
                        f(boT[:, i - 3:i - 1], two(M[1]), ACT.Copy).then_inc(out_free[1], 1)
            memory_attention(1)
            feed_forward(1)
            norm("final", apply=False)

        @block.gpsimd
        def _(pool):
            pool.dma_start(pos_i, a["positions_2"][0].rearrange("(t p) -> p t", p=P), allow_slow_non_contiguous=True).then_inc(sem("pos_in"), 16)

            def gather(rows, slots, here, b, k, used, before, first):
                if not first:
                    pool.wait_ge(used, before)
                    pool.nop(nofuse=True)
                nc.gpsimd.indirect_dma_start(out=slots[k % SLOTS], out_offset=None, in_=rows,
                                             in_offset=bass.IndirectOffsetOnAxis(ap=pidx[:, 16 * b + k:16 * b + k + 1], axis=0)
                                             ).then_inc(here[k % SLOTS], 16)

            def rows_of(g, j, last=False, first=False):
                if not last:
                    pool.wait_ge(sem("topk_done"), g + 2)
                for k in range(PK):
                    if not last:
                        gather(a["peer_u"][0], uslot, u_in, (j + 1) % 4, k, dots_done, 16 * g + 16 + k - 7, False)
                    gather(a["peer_v"][0], vslot, v_in, j, k, v_used, 16 * g + k - 7, first and k < SLOTS)

            pool.wait_ge(sem("topk_done"), 1)
            for k in range(PK):
                gather(a["peer_u"][0], uslot, u_in, 0, k, dots_done, k - 7, k < SLOTS)
            rows_of(0, 0, first=True)
            for j in range(1, 4):
                rows_of(j, j)
            with pool.Fori(1, 3) as i:
                for j in range(4):
                    rows_of(i * 4 + j, j)
            for j in range(4):
                rows_of(12 + j, j, last=(j == 3))

        @block.vector
        def _(dve):
            tt, ts, stt = nc.vector.tensor_tensor, nc.vector.tensor_scalar, nc.vector.scalar_tensor_tensor
            n_steps = [0]

            def link(ins):
                n_steps[0] += 1
                ins.then_inc(steps, 1)
                dve.wait_ge(steps, n_steps[0])

            def turn_copy(n, dst, wait=None):
                dve.wait_ge(turn_ready, n + 1)
                if wait:
                    dve.wait_ge(*wait)
                nc.vector.tensor_copy(dst, like(T[0][:, :], dst)).then_inc(turn_free[0], 1)

            def norm(name, apply=True):
                k, ss, ms, sd, rs = stats(name)
                src, junk, dst = places(name)
                dve.wait_ge(sums_ready, 2 * (k + 1))
                ts(ms, ss, 1.0 / D, EPS, ALU.mult, ALU.add).then_inc(ms_ready, 1)
                dve.wait_ge(sd_ready, k + 1)
                nc.vector.reciprocal(rs, sd).then_inc(rs_ready, 1)
                dve.wait_ge(rs_ready, k + 1)
                if apply:
                    ts(dst[:, 0], src[:, 0], rs[:, 0:1], None, ALU.mult).then_inc(xn_ready[0], 1)

            def turn_scaled(name):
                for u in (0, 2) if turn(name) % 2 == 0 else (1, 3):
                    n = turn(name) + u
                    dve.wait_ge(turn_ready, n + 1)
                    dests = scaled(name)
                    for d, (dst, sc, sh) in enumerate(dests):
                        for cc in range(2):
                            c = 2 * u + cc
                            src = T[0][:, cc * TOK:(cc + 1) * TOK]
                            if sc is None:
                                q = nc.vector.tensor_copy(dst[:, c], src)
                            elif sh is None:
                                q = ts(dst[:, c], src, sc(c), None, ALU.mult)
                            else:
                                q = ts(dst[:, c], src, sc(c), sh(c), ALU.mult, ALU.add)
                            if cc == 1 and d == len(dests) - 1:
                                q.then_inc(turn_free[0], 1)

            nc.vector.memset(ones[:, :], 1.0)
            dve.wait_ge(turn_ready, 1)
            nc.vector.tensor_copy(cols[:, :], T[0][:, 0:184]).then_inc(turn_free[0], 1)
            dve.wait_ge(turn_free[0], 1)
            link(ts(gd, cols[:, C_DN:C_DN + 4], 1.0 - LAM_INIT, None, ALU.mult))
            dve.wait_ge(sem("lg_in"), 16)
            link(nc.vector.tensor_copy(lg, lg_raw8))
            stt(lgt, lg, -1.0, lg, ALU.mult, ALU.max).then_inc(sem("lg_abs"), 1)
            dve.wait_ge(sem("lg_exp"), 1)
            link(ts(lg2, lgt, 1.0, None, ALU.add))
            link(ts(lg3, lg2, -1.0, None, ALU.add))
            link(tt(lg3, lgt, lg3, ALU.subtract))
            link(nc.vector.reciprocal(lg4, lg2))
            tt(lg3, lg3, lg4, ALU.mult).then_inc(sem("lg_one"), 1)
            dve.wait_ge(sem("lg_ln"), 1)
            link(tt(lg2, lg2, lg3, ALU.add))
            stt(lg, lg, 0.0, lg2, ALU.min, ALU.subtract).then_inc(sem("lg_done"), 1)
            dve.wait_ge(sem("lam_in"), 32)
            link(tt(aux[:, 384:448], aux[:, 0:64], aux[:, 64:128], ALU.mult))
            link(nc.vector.reduce_sum(lam2[:, 0:1], aux[:, 384:448], AX))
            link(tt(aux[:, 448:512], aux[:, 128:192], aux[:, 192:256], ALU.mult))
            nc.vector.reduce_sum(lam2[:, 1:2], aux[:, 448:512], AX).then_inc(sem("lam_sums"), 1)
            dve.wait_ge(sem("lam_exp"), 1)
            link(tt(lam, lam2[:, 0:1], lam2[:, 1:2], ALU.subtract))
            link(ts(lam, lam, LAM_INIT, None, ALU.add))
            dve.wait_ge(sem("pos_in"), 16)
            link(nc.vector.tensor_copy(posf, pos_i))
            for t in range(NT):
                link(ts(sinb[:, 16 * t:16 * t + 16], keep[:, K_INV:K_INV + 16], posf[:, t:t + 1], None, ALU.mult))
            big = 12582912.0
            link(ts(cosb, sinb, 1.0 / (2 * math.pi), big, ALU.mult, ALU.add))
            link(ts(cosb, cosb, -big, None, ALU.add))
            for part in TWO_PI:
                link(stt(sinb, cosb, -part, sinb, ALU.mult, ALU.add))
            link(ts(sinb, sinb, PI_F, -PI_F, ALU.min, ALU.max))
            link(stt(cosb, sinb, -1.0, sinb, ALU.mult, ALU.max))
            ts(cosb, cosb, -1.0, math.pi / 2, ALU.mult, ALU.add).then_inc(sem("angles"), 1)
            for u in range(4):
                n = turn("sk") + u
                if n % 2 == 0:
                    turn_copy(n, skT[:, 4 * u:4 * u + 4])
            dve.wait_ge(sem("dist_in"), 16)
            dve.wait_ge(sem("lg_done"), 1)
            for h in range(RH):
                link(ts(dtmp[:, h, 1], dist[:, 2], lg[:, h:h + 1], None, ALU.mult))
                stt(dtmp[:, h, 1], dist[:, 3], lg[:, 4 + h:5 + h], dtmp[:, h, 1], ALU.mult, ALU.add).then_inc(sem("decay_arg"), 1)
                dve.wait_ge(sem("decay_A"), 3 * h + 2)
                link(tt(DEC[:, h, 0:2], DEC[:, h, 0:2], dtmp[:, h, 0], ALU.add))
            def modulation_sums(i):
                n = piece["mod", i]
                w8 = slot8[n % RING]
                parts = [mod_part2(i, 0), mod_part2(i, 1)] if i < 4 else [mod_part(i)]
                dve.wait_ge(landed[n % RING], 32 * (n // RING + 1))
                if i >= 8:
                    dve.wait_ge(sem("mod_done"), i - 3)
                for k in range(KC):
                    for v, part in enumerate(parts):
                        col = cs[:, 8 * v + k:8 * v + k + 1]
                        q = stt(part, w8[:, k], col, part, ALU.mult, ALU.add) if k else ts(part, w8[:, k], col, None, ALU.mult)
                    if k < KC - 1:
                        link(q)
                q.then_inc(sem("mod_sums"), 1)

            dve.wait_ge(sem("c_silu"), 1)
            modulation_sums(1)
            norm("x")
            norm("ctx")
            norm("mem")
            modulation_sums(3)
            bm = cols[:, C_BM:C_BM + 48].unsqueeze(2)
            dve.wait_ge(sem("mod_done"), 4)
            link(tt(mod[:, 0:16], M[1][:, 0:32].rearrange("p (n v) -> p n v", v=2), bm[:, 0:16].to_broadcast([P, 16, 2]), ALU.add))
            link(stt(a_x, mod[:, 8:16, 0], 1.0, cols[:, C_N1:C_N1 + 8], ALU.add, ALU.mult))
            stt(a_c, mod[:, 8:16, 1], 1.0, cols[:, C_N1:C_N1 + 8], ALU.add, ALU.mult).then_inc(sem("mod_cols"), 1)
            dve.wait_ge(sem("mod_cols"), 1)
            turn_scaled("x")
            turn_scaled("ctx")
            turn_scaled("mem")

            def project(name, buf, c, w):
                n = lin(name)
                dve.wait_ge(lin_ready, 2 * n + 1)
                nc.vector.tensor_copy(buf[:, 0, c:c + w], L(n, 0)[:, 0:w]).then_inc(lin_free["D"], 1)

            def both_read(name):
                for w in LINEAR[lin(name)][1]:
                    dve.wait_ge(lin_free[w], freed_after(lin(name), w))

            cosr = keep[:, K_COS:K_COS + 128].rearrange("p (t n) -> p t n", t=NT)
            sinr = keep[:, K_SIN:K_SIN + 128].rearrange("p (t s e n) -> p t s e n", t=NT, s=2, e=2)

            def rope(v, t, groups):
                w = groups * 64
                A = tmpA[:, 0:w]
                B = tmpB[:, 0:w].rearrange("p (g s e n) -> p g s e n", g=groups, s=2, e=2)
                v5 = v.rearrange("p (g s e n) -> p g s e n", g=groups, s=2, e=2)
                tt(A.rearrange("p (g n) -> p g n", g=groups), v.rearrange("p (g n) -> p g n", g=groups),
                   cosr[:, t].unsqueeze(1).to_broadcast([P, groups, 64]), ALU.mult)
                for e in range(2):
                    q = tt(B[:, :, :, e], v5[:, :, :, 1 - e], sinr[:, t, :, e].unsqueeze(1).to_broadcast([P, groups, 2, 16]), ALU.mult)
                link(q)
                tt(v, A, tmpB[:, 0:w], ALU.add).then_inc(sem("roped"), 1)

            gq = aux[:, 256:384].rearrange("p (s n) -> p s n", s=2)

            def group_norm(v, t, groups, c, k, gain, done):
                w = groups * 64
                link(tt(tmpA[:, 0:w], v, v, ALU.mult))
                link(nc.vector.tensor_reduce(dss[:, c:c + groups], tmpA[:, 0:w].rearrange("p (g n) -> p g n", g=groups), AX, ALU.add))
                ts(dms[:, c:c + groups], dss[:, c:c + groups], 1.0 / DD, EPS, ALU.mult, ALU.add).then_inc(sem("dms_ready"), 1)
                dve.wait_ge(sem("dsd_ready"), k)
                link(nc.vector.reciprocal(drs[:, c:c + groups], dsd[:, c:c + groups]))
                v3 = v.rearrange("p (g n) -> p g n", g=groups)
                link(tt(v3, v3, drs[:, c:c + groups].unsqueeze(2).to_broadcast([P, groups, 64]), ALU.mult))
                if groups == 8:
                    q = tt(v3, v3, gain[:, 1].unsqueeze(1).to_broadcast([P, 8, 64]), ALU.mult)
                else:
                    v4 = v.rearrange("p (s g n) -> p s g n", s=2, g=8)
                    q = tt(v4, v4, gain.unsqueeze(2).to_broadcast([P, 2, 8, 64]), ALU.mult)
                if done:
                    q.then_inc(sem("roped"), 1)
                else:
                    link(q)

            for name, buf, c, w in ((("in0", PR, 0, 512), ("in0c", PC, 0, 256), ("in1", PR, 512, 512), ("in1c", PC, 256, 512),
                                    ("in3", PR, 1536, 512), ("in4", PR, 2048, 512), ("in4c", PC, 768, 512),
                                    ("in5", PR, 2560, 512), ("in5c", PC, 1280, 512))):
                project(name, buf, c, w)
                if name == "in1c":
                    both_read("in0")
                    rope(PR[:, 0, 0:512], 0, 8)
                    dve.wait_ge(sem("roped"), 1)
                    rope(PR[:, 1, 0:512], 1, 8)
                    dve.wait_ge(sem("roped"), 2)
                for i in {"in0": (4,), "in0c": (5,), "in1": (6,), "in1c": (7, 8, 9), "in4": (10,), "in4c": (11,)}.get(name, ()):
                    modulation_sums(i)
                if name == "in4c":
                    both_read("in4c")
                    group_norm(PC[:, 0, 768:1280], 0, 8, 0, 1, gq, True)
                    group_norm(PC[:, 1, 768:1280], 1, 8, 8, 2, gq, True)
                    for t in range(NT):
                        v = PR[:, t, 1536:2560]
                        group_norm(v, t, 16, 0, 3 + t, gq, False)
                        rope(v, t, 16)
                        dve.wait_ge(sem("roped"), 5 + t)

            def diag_row(dst, col):
                return tt(dst.rearrange("p (k n) -> p k n", k=KC), ident.unsqueeze(1).to_broadcast([P, KC, P]),
                          col.unsqueeze(2).to_broadcast([P, KC, P]), ALU.mult)

            def row_half(n, dst):
                dve.wait_ge(lin_ready, 2 * n + 1)
                nc.vector.tensor_copy(dst[:, 0:512], L(n, 0)[:, :]).then_inc(lin_free["D"], 1)

            dve.wait_ge(sem("mod_done"), 12)
            link(tt(mod[:, 16:48], M[1][:, 32:96].rearrange("p (n v) -> p n v", v=2), bm[:, 16:48].to_broadcast([P, 32, 2]), ALU.add))
            stt(a_2, mod[:, 32:40, 0], 1.0, cols[:, C_N2:C_N2 + 8], ALU.add, ALU.mult).then_inc(sem("mod_cols"), 1)
            dve.wait_ge(sem("mod_cols"), 2)
            dve.wait_ge(lin_ready, 2 * lin("in5c") + 2)
            diag_row(g2row, mod[:, 16:24, 0]).then_inc(sem("rows_diag"), 1)
            row_half(lin("g2row"), g2row)
            for name in ("rq", "rkc", "rk"):
                if turn(name) % 2 == 0:
                    dst = {"rq": rqT, "rkc": rkT[:, :, 0:TOK], "rk": rkT[:, :, TOK:2 * TOK]}[name]
                    turn_copy(turn(name), dst)
            for name, dst, c0 in (("dkc", dkT, 0), ("dq", dqT, 0), ("dk", dkT, TOK)):
                for u in range(2):
                    if (turn(name) + u) % 2 == 0:
                        turn_copy(turn(name) + u, dst[:, 2 * u:2 * u + 2, c0:c0 + TOK])
            for h in range(RH):
                n = lin("ret") + h
                if h >= 2:
                    dve.wait_ge(sem("ret_out"), h - 1)
                for p in range(2):
                    dve.wait_ge(lin_ready, 2 * n + 1 + p)
                    q = stt(PT[:, h % 2, 2 * p:2 * p + 2].rearrange("p j n -> p (j n)"), L(n, p)[:, :], RDK ** -0.5,
                            DEC[:, h, 2 * p:2 * p + 2].rearrange("p j n -> p (j n)"), ALU.mult, ALU.mult)
                q.then_inc(lin_free["D"], 1)

            def out_norm(k):
                dve.wait_ge(sem("ysum"), k)
                ts(yms, yss, 1.0 / P, EPS, ALU.mult, ALU.add).then_inc(sem("yms"), 1)
                dve.wait_ge(sem("ysd"), k)
                nc.vector.reciprocal(yrs, ysd).then_inc(sem("yrs"), 1)
                dve.wait_ge(sem("yrs"), k)

            out_norm(1)
            for t in range(NT):
                for h in range(RH):
                    q = stt(PR[:, t, h * P:(h + 1) * P], M[t][:, h * P:(h + 1) * P], yrs[:, 4 * t + h:4 * t + h + 1],
                            PR[:, t, 1024 + h * P:1024 + (h + 1) * P], ALU.mult, ALU.mult)
            q.then_inc(sem("mix_D"), 1)

            def diff_max(i):
                n, b = lin("diff") + i, i % 2
                for p in range(2):
                    dve.wait_ge(lin_ready, 2 * n + 1 + p)
                    q = nc.vector.reduce_max(mx[:, 2 * b + p:2 * b + p + 1], L(n, p)[:, :], AX)
                q.then_inc(lin_free["D"], 1)
                dve.wait_ge(lin_free["D"], freed_after(n, "D"))
                ts(nmx[:, 2 * b:2 * b + 2], mx[:, 2 * b:2 * b + 2], -DSCALE, None, ALU.mult).then_inc(nmx_ready, 1)

            def diff_mix(i):
                n, b = lin("diff") + i, i % 2
                dve.wait_ge(lin_free["A"], freed_after(n, "A"))
                link(nc.vector.reciprocal(rz[:, 2 * b:2 * b + 2], zz[:, 2 * b:2 * b + 2]))
                link(ts(rz[:, 2 * b + 1:2 * b + 2], rz[:, 2 * b + 1:2 * b + 2], lam[:, 0:1], None, ALU.mult))
                link(ts(EX[:, b, 1], EX[:, b, 1], rz[:, 2 * b + 1:2 * b + 2], None, ALU.mult))
                stt(EX[:, b, 0], EX[:, b, 0], rz[:, 2 * b:2 * b + 1], EX[:, b, 1], ALU.mult, ALU.subtract).then_inc(probs_ready, 1)

            diff_max(0)
            for i in range(9):
                if i + 1 < 8:
                    diff_max(i + 1)
                if i < 8:
                    diff_mix(i)
                if i >= 1 and (turn("at") + i - 1) % 2 == 0:
                    j = i - 1
                    turn_copy(turn("at") + j, aT[:, j % 2], (sem("diff_out"), j - 1) if j >= 2 else None)
            out_norm(2)
            for h in range(4):
                q = ts(PR[:, 0, 1536 + h * P:1536 + (h + 1) * P], M[0][:, h * P:(h + 1) * P], yrs[:, h:h + 1], None, ALU.mult)
            q.then_inc(sem("mix_D"), 1)
            diag_row(arow, a_2).then_inc(sem("rows_diag"), 1)
            diag_row(brow, mod[:, 24:32, 0]).then_inc(sem("rows_diag"), 1)
            row_half(lin("arow"), arow)
            row_half(lin("brow"), brow)
            turn_scaled("mix")
            dve.wait_ge(lin_free["A"], freed_after(lin("brow"), "A"))
            for half in range(2):
                for t in range(NT):
                    n, c = lin("out") + half, slice(half * 512, (half + 1) * 512)
                    dve.wait_ge(lin_ready, 2 * n + 1 + t)
                    gated = (tmpA, tmpB)[t][:, c]
                    q = tt(gated, L(n, t)[:, :], g2row[:, c], ALU.mult)
                    if t:
                        q.then_inc(lin_free["D"], 1)
                        dve.wait_ge(lin_free["D"], freed_after(n, "D"))
                    else:
                        link(q)
                    tt(x[:, t, c], x[:, t, c], gated, ALU.add).then_inc(x_ready, 1)
            norm("h2", apply=False)
            rs = stats("h2")[4]
            for t in range(NT):
                link(stt(h2[:, t], x[:, t], rs[:, t:t + 1], arow, ALU.mult, ALU.mult))
                tt(h2[:, t], h2[:, t], brow, ALU.add).then_inc(xn_ready[t], 1)
            turn_scaled("h2")
            for c in range(4):
                n = lin("wq") + c
                dve.wait_ge(lin_ready, 2 * n + 1)
                nc.vector.tensor_copy(qT[:, 4 * c:4 * c + 2], two(L(n, 0))).then_inc(lin_free["D"], 1)
            dve.wait_ge(lin_ready, 2 * (lin("wq") + 4))
            diag_row(g5row, mod[:, 40:48, 0]).then_inc(sem("rows_diag"), 1)
            for u in range(4):
                n = lin("key") + u
                dve.wait_ge(lin_ready, 2 * n + 1)
                nc.vector.tensor_copy(s_all[:, u * 1024:u * 1024 + 512], L(n, 0)[:, :]).then_inc(lin_free["D"], 1)
            row_half(lin("g5row"), g5row)
            dve.wait_ge(lin_free["A"], freed_after(lin("g5row"), "A"))

            psteps = sem("peer_steps")
            count = [0, 0]

            def chain(ins):
                count[0] += 1
                ins.then_inc(psteps, 1)
                dve.wait_ge(psteps, count[1] + count[0])
                dve.nop(nofuse=True)

            def top_k(g, b):
                chain(nc.vector.tensor_copy(cur, s_all[:, bass.ds(g * 256, 256)] if not isinstance(g, int) else s_all[:, g * 256:g * 256 + 256]))
                for s in range(2):
                    v, ix, c = top_v[:, 16 * s:16 * s + 16], u_topi[:, 16 * s:16 * s + 16], cur[:, s * P:(s + 1) * P]
                    chain(nc.vector.max(v[:, 0:8], c))
                    chain(nc.vector.max_index(ix[:, 0:8], v[:, 0:8], c))
                    chain(nc.vector.match_replace(c, v[:, 0:8], c, MINF))
                    chain(nc.vector.max(v[:, 8:16], c))
                    chain(nc.vector.max_index(ix[:, 8:16], v[:, 8:16], c))
                chain(nc.vector.tensor_copy(top_i, u_topi))
                cd = cand.rearrange("p (a b) -> p a b", a=16)
                chain(tt(cd, top_v[:, 0:16].unsqueeze(2).to_broadcast([P, 16, 16]), top_v[:, 16:32].unsqueeze(1).to_broadcast([P, 16, 16]), ALU.add))
                best = best4[:, 16 * b:16 * b + 16]
                chain(nc.vector.max(best[:, 0:8], cand))
                chain(nc.vector.max_index(u_pos[:, 0:8], best[:, 0:8], cand))
                chain(nc.vector.match_replace(cand2, best[:, 0:8], cand, MINF))
                chain(nc.vector.max(best[:, 8:16], cand2))
                chain(nc.vector.max_index(u_pos[:, 8:16], best[:, 8:16], cand2))
                chain(ts(nbest4[:, b:b + 1], best[:, 0:1], -1.0, None, ALU.mult))
                chain(ts(u_hl[:, 0:16], u_pos, 4, None, ALU.logical_shift_right))
                chain(ts(u_hl[:, 16:32], u_pos, 15, None, ALU.bitwise_and))
                chain(nc.vector.tensor_copy(top_pos, u_hl))
                h3 = hot.rearrange("p (a b) -> p a b", a=16)
                sel = [top_sel, top_v[:, 0:16]]
                for s in range(2):
                    chain(tt(h3, iota16.unsqueeze(1).to_broadcast([P, 16, 16]), top_pos[:, 16 * s:16 * s + 16].unsqueeze(2).to_broadcast([P, 16, 16]), ALU.is_equal))
                    chain(tt(h3, h3, top_i[:, 16 * s:16 * s + 16].unsqueeze(1).to_broadcast([P, 16, 16]), ALU.mult))
                    chain(nc.vector.tensor_reduce(sel[s], h3, AX, ALU.add))
                stt(pidx[:, 16 * b:16 * b + 16], sel[0], float(PN), sel[1], ALU.mult, ALU.add).then_inc(sem("topk_done"), 1)

            def dots(g, b, tile_h2):
                for k in range(PK):
                    dve.wait_ge(u_in[k % SLOTS], 32 * g + 16 * (k // SLOTS) + 16)
                    stt(uslot[k % SLOTS], uslot[k % SLOTS], 1.0, tile_h2, ALU.mult, ALU.mult,
                        accum_out=pact2[:, 16 * (b % 2) + k:16 * (b % 2) + k + 1]).then_inc(dots_done, 1)

            def expert_weights(g, b):
                dve.wait_ge(sem("gate_exp"), g + 1)
                chain(nc.vector.reciprocal(prz, pz4[:, b:b + 1]))
                dve.wait_ge(sem("gelu_done"), g + 1)
                c = 16 * (b % 2)
                stt(pw2[:, c:c + 16], pgel2[:, c:c + 16], prz, gate4[:, 16 * b:16 * b + 16], ALU.mult, ALU.mult).then_inc(sem("weights_ready"), 1)

            def add_experts(t):
                dve.wait_ge(v_used, 128 * (t + 1))
                acc = (M, T)[t]
                for half in range(2):
                    c = slice(half * 512, (half + 1) * 512)
                    part = h2[:, t, c]
                    chain(tt(part, acc[half][:, :], g5row[:, c], ALU.mult))
                    tt(x[:, t, c], x[:, t, c], part, ALU.add).then_inc(x_ready, 1)

            top_k(0, 0)
            top_k(1, 1)
            pro = count[0]
            PER = pro // 2 + 1
            assert pro % 2 == 0
            with dve.Fori(0, 3) as i:
                for j in range(4):
                    g = i * 4 + j
                    count[0], count[1] = 0, g * PER + pro
                    tile_h2 = h2_all[:, bass.ds((i // 2) * D, D)]
                    dots(g, j, tile_h2)
                    top_k(g + 2, (j + 2) % 4)
                    expert_weights(g, j)
                    assert count[0] == PER
            count[0], count[1] = 0, 12 * PER + pro
            add_experts(0)
            for g in range(12, 16):
                dots(g, g % 4, h2[:, 1])
                if g + 2 < 16:
                    top_k(g + 2, (g + 2) % 4)
                expert_weights(g, g % 4)
            add_experts(1)

            norm("conv")
            turn_scaled("conv")
            for c in range(4):
                n = lin("cb") + c
                dve.wait_ge(lin_ready, 2 * n + 1)
                dst = (bT if c < 2 else cT)[:, 4 * (c % 2):4 * (c % 2) + 2]
                nc.vector.tensor_copy(dst, two(L(n, 0))).then_inc(lin_free["D"], 1)
            link(nc.vector.memset(zT[:, :, 0:2], 0.0))
            dve.wait_ge(lin_free["A"], freed_after(lin("cb") + 3, "A"))
            for u in range(2):
                n = lin("cu") + u
                for b in range(2):
                    dve.wait_ge(lin_ready, 2 * n + 1 + b)
                    c = 4 * u + 2 * b
                    q = tt(zT[:, c:c + 2, 2:2 + TOK], cT[:, c:c + 2], L(n, b)[:, :].rearrange("p (k n) -> p k n", k=2), ALU.mult)
                q.then_inc(lin_free["D"], 1)
                dve.wait_ge(lin_free["D"], freed_after(n, "D"))
                for tap in (1, 2):
                    for c in range(4 * u, 4 * u + 4):
                        if tap == 1:
                            dve.wait_ge(sem("tap0"), c + 1)
                        q = stt(cvT[:, c], zT[:, c, tap:tap + TOK], cols[:, C_CONV + 8 * tap + c:C_CONV + 8 * tap + c + 1], cvT[:, c],
                                ALU.mult, ALU.add)
                    link(q)
                tt(cvT[:, 4 * u:4 * u + 4], cvT[:, 4 * u:4 * u + 4], bT[:, 4 * u:4 * u + 4], ALU.mult).then_inc(sem("conv_done"), 1)

            def residual(name):
                for half in range(2):
                    for t in range(NT):
                        n, c = lin(name) + half, slice(half * 512, (half + 1) * 512)
                        dve.wait_ge(lin_ready, 2 * n + 1 + t)
                        q = tt(x[:, t, c], x[:, t, c], L(n, t)[:, :], ALU.add)
                    q.then_inc(lin_free["D"], 1)

            residual("cout")

            def memory_attention(l):
                norm(f"mem{l}")
                turn_scaled(f"mem{l}")
                for c in range(2):
                    n = lin(f"mq{l}") + c
                    dve.wait_ge(lin_ready, 2 * n + 1)
                    nc.vector.tensor_copy(mqT[:, 4 * c:4 * c + 2], two(L(n, 0))).then_inc(lin_free["D"], 1)

                def maxima(i):
                    n, b = lin(f"ms{l}") + i, i % 2
                    for t in range(NT):
                        dve.wait_ge(lin_ready, 2 * n + 1 + t)
                        q = nc.vector.reduce_max(mx[:, 2 * b + t:2 * b + t + 1], L(n, t)[:, 0:TOK], AX)
                    q.then_inc(lin_free["D"], 1)
                    dve.wait_ge(lin_free["D"], freed_after(n, "D"))
                    ts(nmx[:, 2 * b:2 * b + 2], mx[:, 2 * b:2 * b + 2], -MSCALE, None, ALU.mult).then_inc(nmx_ready, 1)

                maxima(0)
                for i in range(MH + 2):
                    if i + 1 < MH:
                        maxima(i + 1)
                    if i < MH:
                        n, b = lin(f"ms{l}") + i, i % 2
                        dve.wait_ge(lin_free["A"], freed_after(n, "A"))
                        link(nc.vector.reciprocal(rz[:, 2 * b:2 * b + 2], zz[:, 2 * b:2 * b + 2]))
                        for t in range(NT):
                            q = ts(pE[:, b, t], pE[:, b, t], rz[:, 2 * b + t:2 * b + t + 1], None, ALU.mult)
                        q.then_inc(probs_ready, 1)
                    o = out_use(f"om{l}") + i
                    if 1 <= i <= MH and (turn(f"pm{l}") + i - 1) % 2 == 0:
                        turn_copy(turn(f"pm{l}") + i - 1, pT[:, (i - 1) % 2], (out_ready, out_need(o - 3)) if i >= 3 else None)
                    if i >= 2 and (o - 2) % 2 == 0:
                        dve.wait_ge(out_ready, out_need(o - 2))
                        nc.vector.tensor_copy(oT[:, 2 * (i - 2):2 * (i - 2) + 2], two(M[0])).then_inc(out_free[0], 1)
                residual(f"mo{l}")

            def feed_forward(l):
                norm(f"ffn{l}")
                turn_scaled(f"ffn{l}")
                n0 = lin(f"gu{l}")

                def product(j, i=None):
                    n, k = n0 + j, (0 if i is None else i)
                    dve.wait_ge(lin_free["A"], freed_after(n, "A") + 4 * k)
                    dve.wait_ge(lin_ready, 2 * n + 2 + 8 * k)
                    c0 = 4096 + j * 512
                    dst = arena[:, c0:c0 + 512] if i is None else arena[:, bass.ds(i * 2048 + c0, 512)]
                    tt(dst, sg[:, j % 2], L(n, 1)[:, :], ALU.mult).then_inc(lin_free["D"], 1)

                with dve.Fori(0, 2) as i:
                    for j in range(4):
                        product(j, i)
                for j in range(8, 11):
                    product(j)
                residual(f"dn{l}")

            memory_attention(0)
            feed_forward(0)
            norm("blk")
            turn_scaled("blk")
            for name, dst in (("bk", bqk[:, 0, 1]), ("bv", bv[:, 0]), ("bq", bqk[:, 0, 0])):
                for half in range(2):
                    n = lin(name) + half
                    dve.wait_ge(lin_ready, 2 * n + 1)
                    nc.vector.tensor_copy(dst[:, half * 512:(half + 1) * 512], L(n, 0)[:, :]).then_inc(lin_free["D"], 1)
            dve.wait_ge(lin_free["D"], freed_after(lin("bq") + 1, "D"))
            dve.wait_ge(lin_free["A"], freed_after(lin("bq") + 1, "A"))
            dve.wait_ge(sem("sines"), 2)
            for t in range(NT):
                v = bqk[:, t].rearrange("p s (h n) -> p (s h) n", h=BH)
                v1, v2 = v[:, :, 0:16], v[:, :, 16:32]
                co = cosb[:, 16 * t:16 * t + 16].unsqueeze(1).to_broadcast([P, 16, 16])
                si = sinb[:, 16 * t:16 * t + 16].unsqueeze(1).to_broadcast([P, 16, 16])
                tt(rot[:, 0], v2, si, ALU.mult)
                link(tt(rot[:, 1], v1, si, ALU.mult))
                tt(v1, v1, co, ALU.mult)
                link(tt(v2, v2, co, ALU.mult))
                tt(v1, v1, rot[:, 0], ALU.subtract)
                tt(v2, v2, rot[:, 1], ALU.add).then_inc(sem("brot"), 1)
                dve.wait_ge(sem("brot"), t + 1)
            for name, dst in (("bqT", bqT), ("bkT", bkT)):
                for u in range(4):
                    if (turn(name) + u) % 2 == 0:
                        turn_copy(turn(name) + u, dst[:, 2 * u:2 * u + 2])
            tri = keep[:, K_TRI:K_TRI + P]

            def block_max(i):
                n, b = lin("bs") + i, i % 2
                if i >= 2:
                    dve.wait_ge(turn_ready, turn("pb") + i - 1)
                dve.wait_ge(lin_ready, 2 * n + 1)
                stt(bE[:, b, 0, 0:P], L(n, 0)[:, 0:P], BSCALE, tri, ALU.mult, ALU.add)
                dve.wait_ge(lin_ready, 2 * n + 2)
                ts(bE[:, b, 1, 0:P], L(n, 1)[:, 0:P], BSCALE, None, ALU.mult)
                stt(bE[:, b, 1, P:TOK], L(n, 1)[:, P:TOK], BSCALE, tri, ALU.mult, ALU.add).then_inc(lin_free["D"], 1)
                dve.wait_ge(lin_free["D"], freed_after(n, "D"))
                nc.vector.reduce_max(mx[:, 2 * b:2 * b + 1], bE[:, b, 0, 0:P], AX)
                link(nc.vector.reduce_max(mx[:, 2 * b + 1:2 * b + 2], bE[:, b, 1], AX))
                ts(nmx[:, 2 * b:2 * b + 2], mx[:, 2 * b:2 * b + 2], -1.0, None, ALU.mult).then_inc(nmx_ready, 1)

            block_max(0)
            for i in range(BH + 2):
                if i + 1 < BH:
                    block_max(i + 1)
                if i < BH:
                    b = i % 2
                    dve.wait_ge(sem("bexp"), i + 1)
                    link(nc.vector.reciprocal(rz[:, 2 * b:2 * b + 2], zz[:, 2 * b:2 * b + 2]))
                    ts(bE[:, b, 0, 0:P], bE[:, b, 0, 0:P], rz[:, 2 * b:2 * b + 1], None, ALU.mult)
                    ts(bE[:, b, 1], bE[:, b, 1], rz[:, 2 * b + 1:2 * b + 2], None, ALU.mult).then_inc(probs_ready, 1)
                if 1 <= i <= BH and (turn("pb") + i - 1) % 2 == 0:
                    n = turn("pb") + i - 1
                    dve.wait_ge(turn_ready, n + 1)
                    if i >= 3:
                        dve.wait_ge(out_ready, MH + i - 2)
                    nc.vector.tensor_copy(bPT[:, (i - 1) % 2].rearrange("p k n -> p (k n)")[:, 0:3 * P], T[0][:, 0:3 * P]).then_inc(turn_free[0], 1)
                if i >= 2 and i % 2 == 1:
                    o = out_use("ob") + (i - 2) // 2
                    if o % 2 == 0:
                        dve.wait_ge(out_ready, out_need(o))
                        nc.vector.tensor_copy(boT[:, i - 3:i - 1], two(M[0])).then_inc(out_free[0], 1)
            residual("bo")
            memory_attention(1)
            feed_forward(1)
            norm("final", apply=False)
            rs = stats("final")[4]
            dve.wait_ge(sem("frow_in"), 16)
            for t in range(NT):
                stt(h2[:, t], x[:, t], rs[:, t:t + 1], frow, ALU.mult, ALU.mult).then_inc(sem("y_done"), 1)


OUT_SHAPE = (1, TOK, D)


def kernel(**inputs):
    import concourse.bacc as bacc
    from concourse.bass_utils import run_bass_kernel_spmd

    nc = bacc.Bacc("TRN2", target_bir_lowering=False, num_devices=1)
    keep, dist = shape_constants()
    arrays, args = {}, {}
    for name, value in [*inputs.items(), ("keep", keep), ("dist", dist)]:
        v = np.ascontiguousarray(value)
        arrays[f"in_{name}"] = v
        args[name] = nc.dram_tensor(f"in_{name}", v.shape, mybir.dt.from_np(v.dtype), kind="ExternalInput").ap()
    out = nc.dram_tensor("out_y", OUT_SHAPE, F32, kind="ExternalOutput").ap()
    build_program(nc, args, out)
    result = run_bass_kernel_spmd(nc, [arrays], core_ids=[0])
    return result.results[0]["out_y"]
```
